# Optimizing a Trainium2 kernel written in Bass

```python
import jax, jax.numpy as jnp
from jax import lax
import numpy as np

D_MODEL = 2048
BATCH = 1
SEQ = 256
DEPTH = 1

HEAD_DIM = 64
SWA_HEADS = 16
SWA_KV_HEADS = 4
SWA_GROUP = SWA_HEADS // SWA_KV_HEADS
WINDOW = 128
DSA_HEADS = 16
IDX_HEADS = 16
IDX_DIM = 64
DSA_TOPK_MAX = 256
DSA_BLOCK = 128
SWA_Q_WIDTH = SWA_HEADS * HEAD_DIM
SWA_KV_WIDTH = SWA_KV_HEADS * HEAD_DIM
DSA_Q_WIDTH = DSA_HEADS * HEAD_DIM
IDX_Q_WIDTH = IDX_HEADS * IDX_DIM
IN_WIDTH = (SWA_Q_WIDTH + 2 * SWA_KV_WIDTH + DSA_Q_WIDTH + 2 * HEAD_DIM
            + IDX_Q_WIDTH + IDX_DIM + IDX_HEADS + 2 * D_MODEL)
N_ALIBI_HEADS = SWA_HEADS + DSA_HEADS
N_GROUPS = 4
EXPERTS_PER_GROUP = 8
N_EXPERTS = N_GROUPS * EXPERTS_PER_GROUP
EXPERT_TOP_K = 2
D_EXPERT = 512
RMS_EPS = 1e-6
NEG_INF = -1e30

kernel_name = "hybrid_swa_dsa_hmoe_block"

def rms_norm(x, g):
    xf = x.astype(jnp.float32)
    y = xf * lax.rsqrt(jnp.mean(xf * xf, axis=-1, keepdims=True) + RMS_EPS)
    return (y * g.astype(jnp.float32)).astype(x.dtype)

def alibi_slopes():
    i = jnp.arange(1, N_ALIBI_HEADS + 1, dtype=jnp.float32)
    return jnp.exp2(-8.0 * i / N_ALIBI_HEADS)

def swa_sink_attention(q, k, v, sinks, slopes, q_gain, k_gain):
    B, S = q.shape[0], q.shape[1]
    nb = S // WINDOW
    q = rms_norm(q, q_gain)
    k = rms_norm(k, k_gain)
    qb = q.reshape(B, nb, WINDOW, SWA_KV_HEADS, SWA_GROUP, HEAD_DIM)
    pad = jnp.zeros((B, WINDOW, SWA_KV_HEADS, HEAD_DIM), k.dtype)
    kp = jnp.concatenate([pad, k], axis=1)[:, :S]
    vp = jnp.concatenate([pad, v], axis=1)[:, :S]
    blk = (B, nb, WINDOW, SWA_KV_HEADS, HEAD_DIM)
    kw = jnp.concatenate([kp.reshape(blk), k.reshape(blk)], axis=2)
    vw = jnp.concatenate([vp.reshape(blk), v.reshape(blk)], axis=2)
    scale = HEAD_DIM ** -0.5
    s = jnp.einsum('bnqkgd,bnskd->bnkgqs', qb, kw).astype(jnp.float32) * scale
    rel = (jnp.arange(WINDOW)[:, None] + WINDOW - jnp.arange(2 * WINDOW)[None, :])
    kpos = jnp.arange(nb)[:, None] * WINDOW - WINDOW + jnp.arange(2 * WINDOW)[None, :]
    valid = ((rel >= 0) & (rel < WINDOW))[None] & (kpos >= 0)[:, None, :]
    sl = slopes.reshape(SWA_KV_HEADS, SWA_GROUP)[:, :, None, None]
    s = s - sl * rel.astype(jnp.float32)
    s = jnp.where(valid[None, :, None, None], s, NEG_INF)
    sink = sinks.astype(jnp.float32).reshape(SWA_KV_HEADS, SWA_GROUP)[None, None, :, :, None, None]
    m = jnp.maximum(jnp.max(s, axis=-1, keepdims=True), sink)
    e = jnp.exp(s - m)
    p = (e / (jnp.sum(e, axis=-1, keepdims=True) + jnp.exp(sink - m))).astype(v.dtype)
    o = jnp.einsum('bnkgqs,bnskd->bnqkgd', p, vw)
    return o.reshape(B, S, SWA_Q_WIDTH)

def dsa_attention(q, k, v, qi, ki, wi, slopes, q_gain, k_gain):
    B, S = q.shape[0], q.shape[1]
    topk = min(DSA_TOPK_MAX, S // 4)
    nb = S // DSA_BLOCK
    q = rms_norm(q, q_gain)
    k = rms_norm(k, k_gain)
    kif = ki.astype(jnp.float32)
    kpos = jnp.arange(S)
    scale = HEAD_DIM ** -0.5
    sl = slopes.astype(jnp.float32)[None, :, None, None]

    def to_blocks(a):
        return a.reshape((B, nb, DSA_BLOCK) + a.shape[2:]).swapaxes(0, 1)

    def block_fn(args):
        qb, qib, wib, start = args
        t = start + jnp.arange(DSA_BLOCK)
        logits = jnp.einsum('bqhd,bsd->bqhs', qib.astype(jnp.float32), kif) * IDX_DIM ** -0.5
        w = wib.astype(jnp.float32) * IDX_HEADS ** -0.5
        score = jnp.einsum('bqhs,bqh->bqs', jax.nn.relu(logits), w)
        causal = kpos[None, :] <= t[:, None]
        score = jnp.where(causal[None], score, -jnp.inf)
        _, idx = lax.top_k(score, topk)
        kg = jax.vmap(lambda kk, ii: kk[ii])(k, idx)
        vg = jax.vmap(lambda vv, ii: vv[ii])(v, idx)
        dist = t[None, :, None] - idx
        s = jnp.einsum('bqhd,bqkd->bhqk', qb, kg).astype(jnp.float32) * scale
        s = s - sl * dist[:, None].astype(jnp.float32)
        s = jnp.where((dist >= 0)[:, None], s, NEG_INF)
        p = jax.nn.softmax(s, axis=-1).astype(vg.dtype)
        return jnp.einsum('bhqk,bqkd->bqhd', p, vg)

    starts = jnp.arange(nb) * DSA_BLOCK
    o = lax.map(block_fn, (to_blocks(q), to_blocks(qi), to_blocks(wi), starts))
    return o.swapaxes(0, 1).reshape(B, S, DSA_Q_WIDTH)

def hybrid_mixer(h, slopes, w_in, swa_q_norm, swa_k_norm, swa_sinks, dsa_q_norm, dsa_k_norm,
                 w_branch_a, w_branch_b, w_out):
    B, S, _ = h.shape
    proj = h @ w_in
    sizes = [SWA_Q_WIDTH, SWA_KV_WIDTH, SWA_KV_WIDTH, DSA_Q_WIDTH, HEAD_DIM, HEAD_DIM,
             IDX_Q_WIDTH, IDX_DIM, IDX_HEADS, D_MODEL, D_MODEL]
    offs = np.cumsum(sizes)[:-1].tolist()
    qa, ka, va, qb, kb, vb, qi, ki, wi, ga, gb = jnp.split(proj, offs, axis=-1)
    oa = swa_sink_attention(qa.reshape(B, S, SWA_HEADS, HEAD_DIM),
                            ka.reshape(B, S, SWA_KV_HEADS, HEAD_DIM),
                            va.reshape(B, S, SWA_KV_HEADS, HEAD_DIM),
                            swa_sinks, slopes[:SWA_HEADS], swa_q_norm, swa_k_norm)
    ob = dsa_attention(qb.reshape(B, S, DSA_HEADS, HEAD_DIM), kb, vb,
                       qi.reshape(B, S, IDX_HEADS, IDX_DIM), ki, wi,
                       slopes[SWA_HEADS:], dsa_q_norm, dsa_k_norm)
    merged = jax.nn.sigmoid(ga) * (oa @ w_branch_a) + jax.nn.sigmoid(gb) * (ob @ w_branch_b)
    return merged @ w_out

def hier_moe(h, w_group, b_group, w_expert, b_expert, w_gate_up, w_up, w_down):
    B, S, D = h.shape
    hf = h.reshape(B * S, D)
    g_logits = (hf @ w_group).astype(jnp.float32) + b_group.astype(jnp.float32)
    g_prob = jax.nn.softmax(g_logits, axis=-1)
    g_idx = jnp.argmax(g_logits, axis=-1)
    p_g = jnp.take_along_axis(g_prob, g_idx[:, None], axis=1)[:, 0]
    e_logits = ((hf @ w_expert).astype(jnp.float32) + b_expert.astype(jnp.float32)
                ).reshape(-1, N_GROUPS, EXPERTS_PER_GROUP)
    e_sel = jnp.take_along_axis(e_logits, g_idx[:, None, None], axis=1)[:, 0]
    e_prob = jax.nn.softmax(e_sel, axis=-1)
    top_p, top_i = lax.top_k(e_prob, EXPERT_TOP_K)
    top_p = top_p / jnp.sum(top_p, axis=-1, keepdims=True)
    local = jnp.sum(jax.nn.one_hot(top_i, EXPERTS_PER_GROUP, dtype=jnp.float32) * top_p[..., None], axis=1)
    comb = (jax.nn.one_hot(g_idx, N_GROUPS, dtype=jnp.float32)[:, :, None]
            * (p_g[:, None] * local)[:, None, :]).astype(h.dtype)
    out = jnp.zeros_like(hf)
    for g in range(N_GROUPS):
        a = jnp.einsum('nd,edf->nef', hf, w_gate_up[g])
        u = jnp.einsum('nd,edf->nef', hf, w_up[g])
        act = jax.nn.silu(a) * u * comb[:, g, :, None]
        out = out + jnp.einsum('nef,efd->nd', act, w_down[g])
    return out.reshape(B, S, D)

def setup_inputs(seed: int = 0) -> dict:
    key = jax.random.key(seed)
    ks = jax.random.split(key, 24)
    f32 = jnp.float32
    L, D, F = DEPTH, D_MODEL, D_EXPERT

    def nrm(k, shape, scale):
        return jax.random.normal(k, shape, f32) * scale

    return {
        "x": nrm(ks[0], (BATCH, SEQ, D), 1.0),
        "c": nrm(ks[1], (BATCH, D), 1.0),
        "w_ada": nrm(ks[2], (L, D, 6 * D), 0.5 * D ** -0.5),
        "b_ada": nrm(ks[3], (L, 6 * D), 0.01),
        "ln1_g": 1.0 + nrm(ks[4], (L, D), 0.02),
        "w_in": nrm(ks[5], (L, D, IN_WIDTH), D ** -0.5),
        "swa_q_norm": 1.0 + nrm(ks[6], (L, HEAD_DIM), 0.02),
        "swa_k_norm": 1.0 + nrm(ks[7], (L, HEAD_DIM), 0.02),
        "swa_sinks": nrm(ks[8], (L, SWA_HEADS), 0.5),
        "dsa_q_norm": 1.0 + nrm(ks[9], (L, HEAD_DIM), 0.02),
        "dsa_k_norm": 1.0 + nrm(ks[10], (L, HEAD_DIM), 0.02),
        "w_branch_a": nrm(ks[11], (L, SWA_Q_WIDTH, D), SWA_Q_WIDTH ** -0.5),
        "w_branch_b": nrm(ks[12], (L, DSA_Q_WIDTH, D), DSA_Q_WIDTH ** -0.5),
        "w_out": nrm(ks[13], (L, D, D), D ** -0.5),
        "ln2_g": 1.0 + nrm(ks[14], (L, D), 0.02),
        "w_group": nrm(ks[15], (L, D, N_GROUPS), D ** -0.5),
        "b_group": nrm(ks[16], (L, N_GROUPS), 0.01),
        "w_expert": nrm(ks[17], (L, D, N_EXPERTS), D ** -0.5),
        "b_expert": nrm(ks[18], (L, N_EXPERTS), 0.01),
        "w_gate_up": nrm(ks[19], (L, N_GROUPS, EXPERTS_PER_GROUP, D, F), D ** -0.5),
        "w_up": nrm(ks[20], (L, N_GROUPS, EXPERTS_PER_GROUP, D, F), D ** -0.5),
        "w_down": nrm(ks[21], (L, N_GROUPS, EXPERTS_PER_GROUP, F, D), F ** -0.5),
    }

def reference(x, c, w_ada, b_ada, ln1_g, w_in, swa_q_norm, swa_k_norm, swa_sinks,
              dsa_q_norm, dsa_k_norm, w_branch_a, w_branch_b, w_out, ln2_g,
              w_group, b_group, w_expert, b_expert, w_gate_up, w_up, w_down):
    slopes = alibi_slopes()
    cond = jax.nn.silu(c)
    for l in range(DEPTH):
        mod = (cond @ w_ada[l] + b_ada[l])[:, None, :]
        sh1, sc1, gt1, sh2, sc2, gt2 = jnp.split(mod, 6, axis=-1)
        h = rms_norm(x, ln1_g[l]) * (1.0 + sc1) + sh1
        x = x + gt1 * hybrid_mixer(h, slopes, w_in[l], swa_q_norm[l], swa_k_norm[l], swa_sinks[l],
                                   dsa_q_norm[l], dsa_k_norm[l], w_branch_a[l], w_branch_b[l], w_out[l])
        h = rms_norm(x, ln2_g[l]) * (1.0 + sc2) + sh2
        x = x + gt2 * hier_moe(h, w_group[l], b_group[l], w_expert[l], b_expert[l],
                               w_gate_up[l], w_up[l], w_down[l])
    return x


_drawn_inputs = setup_inputs


def setup_inputs(seed=0):
    import zlib

    import numpy as np

    out = dict(_drawn_inputs(seed))
    spreads = {}
    factors = {'b_ada': 4.53,
     'ln1_g': 6.458,
     'swa_q_norm': 8.0,
     'swa_k_norm': 8.0,
     'swa_sinks': 33.111,
     'dsa_q_norm': 8.0,
     'dsa_k_norm': 8.0,
     'ln2_g': 4.534,
     'b_group': 8.0,
     'b_expert': 8.0}
    for name, (base, spread) in spreads.items():
        noise = np.random.default_rng([zlib.crc32(name.encode()), seed]).standard_normal(out[name].shape)
        drawn = base * np.exp(spread * noise) if base else spread * noise
        out[name] = __import__('jax').numpy.asarray(drawn.astype(out[name].dtype))
    for name, factor in factors.items():
        out[name] = (out[name] * factor).astype(out[name].dtype)
    return out
```

```python
from contextlib import ExitStack


import numpy as np
import concourse.bass as bass
from concourse import mybir

F32 = mybir.dt.float32
I32 = mybir.dt.int32
ALU = mybir.AluOpType
ACT = mybir.ActivationFunctionType
AX = mybir.AxisListType.X

P = 128
D = 2048
SEQ = 256
NT = SEQ // P
HD = 64
NH = 16
KVH = 4
GQ = 4
TOPK = min(256, SEQ // 4)
KC = D // P
NC4 = KC // 4
QA, KA, VA = 0, 1024, 1280
QB, KB, VB = 1536, 2560, 2624
QI, KI, WI = 2688, 3712, 3776
PROJ = 3792
IN_W = PROJ + 2 * D
UW = PROJ // 4
GW = 1024
N_UNITS_PROJ = PROJ // UW
N_UNITS_GATE = 2 * D // GW
RING = 8
RING_MOE = 12
SLOT = 2048
NG, EPG = 4, 8
NE = NG * EPG
FE = 512
EPS = 1e-6
FAR = 1.0e32
NONCAUSAL = -3.0e38
TAKEN = -3.3e38



def slope(i):
    return 2.0 ** (-8.0 * (i + 1) / (2 * NH))


def decoder_block(nc, x, c, w_ada, b_ada, ln1_g, w_in, swa_q_norm, swa_k_norm, swa_sinks,
                  dsa_q_norm, dsa_k_norm, w_branch_a, w_branch_b, w_out, ln2_g, w_group, b_group,
                  w_expert, b_expert, w_gate_up, w_up, w_down, out):
    x_v = x[0].rearrange("(t p) d -> p t d", p=P)
    out_v = out[0].rearrange("(t p) d -> p t d", p=P)
    ada_v = w_ada[0].rearrange("(c p j) n -> p c j n", p=P, j=4)
    in_v = w_in[0].rearrange("(c p j) n -> p c j n", p=P, j=4)
    branch_v = [w[0].rearrange("(k p) n -> p k n", p=P) for w in (w_branch_a, w_branch_b)]
    wo_v = w_out[0].rearrange("(c p j) n -> p c j n", p=P, j=4)
    gate_v = w_gate_up[0].rearrange("g e (c p j) f -> p (g e) c j f", p=P, j=4)
    up_v = w_up[0].rearrange("g e (c p j) f -> p (g e) c j f", p=P, j=4)
    down_v = w_down[0].rearrange("g e (k p) d -> p (g e) k d", p=P)
    bias_v = b_ada[0].rearrange("(s c p j) -> p s c j", s=6, p=P, j=4)

    ctx = ExitStack()
    with ctx:
        def sb(name, shape, dt=F32):
            return ctx.enter_context(nc.sbuf_tensor(name, shape, dt))

        def sem(name):
            return ctx.enter_context(nc.semaphore(name))

        ring = sb("ring", [P, RING, SLOT])
        ada_ring = sb("ada_ring", [P, 2, SLOT])
        hT = sb("hT", [P, KC, SEQ])
        proj = sb("proj", [P, NT, PROJ])
        gates = sb("gates", [P, NT, 2 * D])
        ada_a = sb("ada_a", [P, D])
        ada_b = sb("ada_b", [P, D])
        scratch = sb("scratch", [P, 2 * GQ * SEQ])
        stage = sb("stage", [P, 2, GQ * HD])
        qT = sb("qT", [HD, GQ * P])
        kT = sb("kT", [HD, 2 + KVH, SEQ])
        ident = sb("ident", [P, P])
        ones = sb("ones", [P, P])
        tri = sb("tri", [P, P])
        iota = sb("iota", [P, P])
        rel_swa = sb("rel_swa", [P, SEQ])
        rel_dsa = sb("rel_dsa", [P, SEQ])
        causal = sb("causal", [P, SEQ])
        rel_top = sb("rel_top", [P, NT, SEQ])
        score = sb("score", [P, NT, SEQ])
        top8 = sb("top8", [P, 8])
        nslope = sb("nslope", [P, 2 * NH])
        sinks = sb("sinks", [P, NH])
        wi4 = sb("wi4", [P, NT, NH])
        condr = sb("condr", [P, KC])
        cond = sb("cond", [P, KC])
        cols = sb("cols", [P, 10, KC])
        (C_LN1, C_BSH1, C_BSC1, C_LN2, C_BSH2, C_BSC2, C_A1, C_S1, C_A2, C_S2) = range(10)
        gain_in = sb("gain_in", [HD, 4])
        gain_k = sb("gain_k", [HD, 2])
        stat = sb("stat", [P, 6])
        N_RMS = 2 * NH + KVH + 1
        mhalf = sb("mhalf", [P, 1])
        qk_rstd = sb("qk_rstd", [P, NT, N_RMS])
        kn = sb("kn", [P, NT, (1 + KVH) * HD])
        sm = sb("sm", [P, 7, GQ])
        w_route = sb("w_route", [P, KC, NG + NE])
        b_route = sb("b_route", [P, NG + NE])
        firstw = sb("firstw", [P, 8])
        rt = rel_top[:, :, :].rearrange("p t (i e) -> p (t i) e", e=NT * 8)[:, 0:16, :].rearrange(
            "p i (t e) -> p i t e", t=NT)
        lg = score[:, 0, 0:NT * (NG + NE)].rearrange("p (t n) -> p t n", t=NT)
        esel = score[:, 1, 0:NT * NE].rearrange("p (t n) -> p t n", t=NT)
        onehot = sb("onehot", [P, NT, NG])
        comb = sb("comb", [P, NT, NE])
        rank = sb("rank", [P, NT, NG])
        cnt = sb("cnt", [P, 1])
        flag = sb("flag", [P, 1], I32)
        x1 = proj[:, :, 0:D]
        y_sb = ada_a
        gt2 = ada_b
        hG = hT[:, 0:8, :].rearrange("p a (b s) -> p (a b) s", b=2)
        act_e, act_t, act_o, actT = (scratch[:, FE * i:FE * i + FE] for i in range(4))
        left = [proj[:, t, D:PROJ] for t in range(NT)]
        hot_s = left[0][:, 0:2 * P].rearrange("p (t s) -> p t s", t=NT)
        hot = left[0][:, 2 * P:4 * P].rearrange("p (t s) -> p t s", t=NT)
        hotT = left[1][:, 0:SEQ]
        comb_s = left[1][:, SEQ:SEQ + EPG]
        tmp = left[1][:, SEQ + EPG:SEQ + EPG + 512]
        moe_hi = gates[:, :, :].rearrange("p t (s n) -> p (t s) n", n=SLOT)

        def moe_slot(q):
            return ring[:, q, :] if q < RING else moe_hi[:, q - RING, :]

        bank = [ctx.enter_context(nc.psum_tensor(f"bank{i}", [P, 512], F32)) for i in range(8)]

        in_c, in_x, in_small, in_brow, in_x1, stored = map(
            sem, ("in_c", "in_x", "in_small", "in_brow", "in_x1", "stored"))
        landed = [sem(f"landed{q}") for q in range(RING_MOE)]
        ada_landed = [sem("ada_landed0"), sem("ada_landed1")]
        consts, rstd_ok, qk_pow, staged = map(sem, ("consts", "rstd_ok", "qk_pow", "staged"))
        ada0_used, ada_used, ada_red, ada_done = map(sem, ("ada0_used", "ada_used", "ada_red", "ada_done"))
        w_used, unit_bank, unit_out = map(sem, ("w_used", "unit_bank", "unit_out"))
        silu_e, sq_done, ms_ok, xhat_ok, xT_bank, xT_out, h_ready = map(
            sem, ("silu_e", "sq_done", "ms_ok", "xhat_ok", "xT_bank", "xT_out", "h_ready"))
        kT_bank, kT_out, k_norm, qk_ms, qT_bank, qT_out = map(
            sem, ("kT_bank", "kT_out", "k_norm", "qk_ms", "qT_bank", "qT_out"))
        s_bank, relu_out, relu_used, max_ok, exp_ok = map(
            sem, ("s_bank", "relu_out", "relu_used", "max_ok", "exp_ok"))
        pT_bank, pT_out, o_bank, o_out = map(sem, ("pT_bank", "pT_out", "o_bank", "o_out"))
        t_bank, t_out, merged, x1_ok = map(sem, ("t_bank", "t_out", "merged", "x1_ok"))
        diag_ok, h2_bank, h2_out, logit_bank, r_sub, r_exp, onehot_ok, rank_bank, route_ok = map(
            sem, ("diag_ok", "h2_bank", "h2_out", "logit_bank", "r_sub", "r_exp", "onehot_ok", "rank_bank",
                  "route_ok"))
        g_hot, g_bank, g_out, g_hotT, g_hotT_out = map(
            sem, ("g_hot", "g_bank", "g_out", "g_hotT", "g_hotT_out"))
        gu_used, d_used, e_exp, e_act, e_tr, e_trout = map(
            sem, ("gu_used", "d_used", "e_exp", "e_act", "e_tr", "e_trout"))
        y_bank, y_out, sc_bank, sc_out = map(sem, ("y_bank", "y_out", "sc_bank", "sc_out"))
        dve_own, pool_own = map(sem, ("dve_own", "pool_own"))

        block = ctx.enter_context(nc.Block())
        CREDIT = 1
        ROUND0 = 4
        UNITS = N_UNITS_PROJ + N_UNITS_GATE
        DENSE_ROUNDS = UNITS + 2 + 2
        BRANCH0 = UNITS
        OUT0 = BRANCH0 + 4
        IDX_STEPS = 2 * NT * 2
        ATT_STEPS = 2 * NT * (NH // GQ)
        SMALL = 16 * 21

        class Own:

            def __init__(self, eng, own_sem):
                self.eng, self.sem, self.start, self.n = eng, own_sem, 0, 0

            def add(self, ins):
                ins.then_inc(self.sem, 1)
                self.n += 1

            def wait(self):
                self.eng.wait_ge(self.sem, self.start + self.n)

            def enter(self, i, each):
                self.outer = (self.start, self.n)
                self.start, self.n = self.start + self.n + i * each, 0

            def leave(self, times, each):
                assert self.n == each, (self.n, each)
                start, n = self.outer
                self.start, self.n = start, n + times * each

        @block.sync
        def _(sp):
            def pair(i, half):
                return ring[:, i, 0:4 * half].rearrange("p (j n) -> p j n", j=2)

            def w_ada_piece(n, c_, j, section):
                sp.dma_start(ada_ring[:, n, :], ada_v[:, c_, j, section * D:(section + 1) * D]
                             ).then_inc(ada_landed[n], 16)

            for s in range(2):
                for h in range(2):
                    for i in range(RING):
                        if s + h:
                            sp.wait_ge(ada0_used, CREDIT + (2 * s + h - 1) * RING + i + 1)
                        sp.dma_start(ring[:, i, :], ada_v[:, 2 * h + i // 4, i % 4, s * D:(s + 1) * D]
                                     ).then_inc(landed[i], 16)
            for u in range(N_UNITS_PROJ):
                c0 = PROJ - UW * (u + 1)
                for i in range(RING):
                    if u == 0:
                        sp.wait_ge(ada0_used, CREDIT + 3 * RING + i + 1)
                    else:
                        sp.wait_ge(w_used, (u - 1) * RING + i + 1)
                    sp.dma_start(pair(i, UW // 2), in_v[:, i // 2, 2 * (i % 2):2 * (i % 2) + 2, c0:c0 + UW]
                                 ).then_inc(landed[i], 16)
                    n = u * RING + i
                    if n >= 2:
                        sp.wait_ge(ada_used, CREDIT + n - 1)
                    w_ada_piece(n % 2, n % KC // 4, n % 4, 2 + n // KC)
            with sp.Fori(0, N_UNITS_GATE) as u:
                for i in range(RING):
                    sp.wait_ge(w_used, u * RING + ((N_UNITS_PROJ - 1) * RING + i + 1))
                    sp.dma_start(pair(i, GW // 2),
                                 in_v[:, i // 2, 2 * (i % 2):2 * (i % 2) + 2, bass.ds(u * GW + PROJ, GW)]
                                 ).then_inc(landed[i], 16)
                    if i % 2:
                        m = i // 2
                        sp.wait_ge(ada_used, CREDIT + u * 4 + (2 * KC + m - 1))
                        sp.dma_start(ada_ring[:, m % 2, :],
                                     ada_v[:, bass.ds(u, 1), m, 4 * D:5 * D].rearrange("p a n -> p (a n)")
                                     ).then_inc(ada_landed[m % 2], 16)
            for rnd in range(4):
                for i in range(RING):
                    sp.wait_ge(w_used, (UNITS + rnd - 1) * RING + i + 1)
                    if rnd < 2:
                        u, k = i // 4, 2 * (i % 4)
                        src = branch_v[rnd][:, k:k + 2, u * GW:(u + 1) * GW]
                    else:
                        src = wo_v[:, i // 2, 2 * (i % 2):2 * (i % 2) + 2, (rnd - 2) * GW:(rnd - 1) * GW]
                    sp.dma_start(pair(i, GW // 2), src).then_inc(landed[i], 16)
                    if i % 2:
                        k = 4 * rnd + i // 2
                        sp.wait_ge(ada_used, CREDIT + 3 * KC + k - 1)
                        w_ada_piece(k % 2, k // 4, k % 4, 5)

            def gate_up_pieces(e, wait):
                for q in range(RING):
                    wait(q)
                    src = (gate_v if q < 4 else up_v)[:, e, q % 4, :, :]
                    sp.dma_start(moe_slot(q).rearrange("p (j f) -> p j f", j=4), src).then_inc(landed[q], 16)

            def down_pieces(e, wait):
                for m in range(4):
                    wait(m)
                    sp.dma_start(moe_slot(RING + m), down_v[:, e, m, :]).then_inc(landed[RING + m], 16)

            def one(i):
                return bass.ds(i, 1)

            def gu_dyn(e, base):
                for q in range(RING):
                    sp.wait_ge(gu_used, e * 8 + (8 * (base - 1) + q + 1))
                    v = (gate_v if q < 4 else up_v)[:, one(e), q % 4, :, :].rearrange("p a j f -> p (a j) f")
                    sp.dma_start(moe_slot(q).rearrange("p (j f) -> p j f", j=4), v).then_inc(landed[q], 16)

            def down_dyn(e, base):
                for m in range(4):
                    sp.wait_ge(d_used, e * 4 + (4 * (base - 1) + m + 1))
                    sp.dma_start(moe_slot(RING + m), down_v[:, one(e), m, :].rearrange("p a d -> p (a d)")
                                 ).then_inc(landed[RING + m], 16)

            gate_up_pieces(0, lambda q: sp.wait_ge(w_used, (DENSE_ROUNDS - 1) * RING + q + 1))
            sp.wait_ge(t_bank, 16)
            down_pieces(0, lambda m: None)
            gate_up_pieces(1, lambda q: sp.wait_ge(gu_used, q + 1))
            with sp.Fori(1, NE - 1) as e:
                gu_dyn(e + 1, 0)
                down_dyn(e, 0)
            down_pieces(NE - 1, lambda m: sp.wait_ge(d_used, 4 * (NE - 2) + m + 1))

            sp.wait_ge(route_ok, 1)
            over = sp.value_load(flag[0:1, 0:1], min_val=0, max_val=1)
            with sp.If(over > 0):
                gate_up_pieces(0, lambda q: sp.wait_ge(gu_used, 8 * (NE - 1) + q + 1))
                with sp.Fori(0, NE - 1) as e:
                    gu_dyn(e + 1, NE)
                    down_dyn(e, NE)
                down_pieces(NE - 1, lambda m: sp.wait_ge(d_used, 4 * (2 * NE - 2) + m + 1))
                sp.wait_ge(sc_out, CREDIT + 2 * 8 * NG)
                sp.nop()
            sp.wait_ge(sc_out, CREDIT + 8 * NG)
            for t in range(NT):
                sp.dma_start(out_v[:, t, :], x1[:, t, :]).then_inc(stored, 16)
            sp.wait_ge(stored, 16 * NT)

        @block.gpsimd
        def _(pool):
            own = Own(pool, pool_own)

            def link(ins):
                own.add(ins)
                own.wait()

            link(nc.gpsimd.memset(ident[:, :], 0.0))
            nc.gpsimd.memset(ada_a[:, :], 0.0)
            nc.gpsimd.memset(ada_b[:, :], 0.0)
            nc.gpsimd.affine_select(out=ident[:, :], in_=ident[:, :], compare_op=ALU.not_equal, fill=1.0, base=0,
                                    pattern=[[-1, P]], channel_multiplier=1).then_inc(consts, 1)
            nc.gpsimd.memset(ones[:, :], 1.0).then_inc(consts, 1)
            link(nc.gpsimd.memset(mhalf[:, :], -0.5))
            pool.wait_ge(ms_ok, 1)
            nc.gpsimd.tensor_tensor(stat[:, 4:6], stat[:, 2:4], mhalf[:, 0:1].broadcast_to([P, NT]), ALU.pow).then_inc(rstd_ok, 1)

            for h in range(2 * NH):
                nc.gpsimd.memset(nslope[:, h:h + 1], -slope(h))
            for i in range(8):
                nc.gpsimd.memset(firstw[:, i:i + 1], float(8 - i))
            link(nc.gpsimd.iota(rel_dsa[:, :], pattern=[[-1, SEQ]], base=P, channel_multiplier=1,
                                allow_small_or_imprecise_dtypes=True))
            link(nc.gpsimd.affine_select(out=rel_swa[:, :], in_=rel_dsa[:, :], compare_op=ALU.is_ge, fill=FAR,
                                         base=-1, pattern=[[1, SEQ]], channel_multiplier=-1))
            link(nc.gpsimd.affine_select(out=rel_swa[:, :], in_=rel_swa[:, :], compare_op=ALU.is_ge, fill=FAR,
                                         base=P, pattern=[[-1, SEQ]], channel_multiplier=1))
            link(nc.gpsimd.affine_select(out=rel_dsa[:, :], in_=rel_dsa[:, :], compare_op=ALU.is_ge, fill=FAR,
                                         base=P, pattern=[[-1, SEQ]], channel_multiplier=1))
            link(nc.gpsimd.memset(causal[:, :], 3.0e38))
            link(nc.gpsimd.affine_select(out=causal[:, :], in_=causal[:, :], compare_op=ALU.is_ge, fill=NONCAUSAL,
                                         base=P, pattern=[[-1, SEQ]], channel_multiplier=1))
            link(nc.gpsimd.memset(tri[:, :], 1.0))
            link(nc.gpsimd.affine_select(out=tri[:, :], in_=tri[:, :], compare_op=ALU.is_ge, fill=0.0, base=0,
                                         pattern=[[1, P]], channel_multiplier=-1))
            nc.gpsimd.memset(score[:, :, :], 0.0)
            nc.gpsimd.iota(iota[:, :], pattern=[[1, P]], base=0, channel_multiplier=0,
                           allow_small_or_imprecise_dtypes=True).then_inc(consts, 1)

            pool.wait_ge(unit_out, 8)
            with pool.Fori(0, NH // GQ) as g:
                for t in range(NT):
                    pool.wait_ge(qT_bank, CREDIT + g * 2 + t)
                    nc.gpsimd.tensor_copy(stage[:, t, :], proj[:, t, bass.ds(g * (GQ * HD) + QI, GQ * HD)]
                                          ).then_inc(staged, 1)
            pool.wait_ge(qk_ms, 1)
            v = qk_rstd[:, :, :].rearrange("p t h -> p (t h)")
            nc.gpsimd.tensor_tensor(v, v, mhalf[:, 0:1].broadcast_to([P, NT * N_RMS]), ALU.pow).then_inc(qk_pow, 1)
            pool.wait_ge(ms_ok, 2)
            nc.gpsimd.tensor_tensor(stat[:, 4:6], stat[:, 2:4], mhalf[:, 0:1].broadcast_to([P, NT]), ALU.pow).then_inc(rstd_ok, 1)

        def chunk_cols(v, c_, j):
            return v[:, 512 * c_:512 * c_ + 512].rearrange("p (q j) -> p j q", j=4)[:, j, :]

        @block.tensor
        def _(pe):
            for credited in (qT_bank, e_tr):
                pe.sem_inc(credited, CREDIT)

            def reduce_to_columns(acc, b, o):
                for k in range(KC):
                    mm = nc.tensor.matmul(bank[b][:, o + k:o + k + 1], chunk_cols(acc, k // 4, k % 4), ones[:, 0:1],
                                          start=True, stop=True)
                mm.then_inc(ada_red, 1)

            def reduce_to_rows(acc):
                for q in range(4):
                    nc.tensor.matmul(bank[4 + q][:, :], ones[:, :], acc[:, q * 512:(q + 1) * 512],
                                     start=True, stop=False)
                    mm = nc.tensor.matmul(bank[4 + q][:, :], ones[0:1, :], scratch[0:1, q * 512:(q + 1) * 512],
                                          start=False, stop=True)
                mm.then_inc(ada_red, 1)

            def chunk(rnd, unit, k, half, banks=range(4), slot0=0, lhs0=0, nk=KC):
                i, kk = slot0 + k // 2, k % 2
                if kk == 0 and banks[0] == 0:
                    pe.wait_ge(landed[i], rnd * 16 + 16 * (ROUND0 + 1))
                w = ring[:, i, 0:4 * half].rearrange("p (j n) -> p j n", j=2)
                for b in banks:
                    t, cb = b // 2, b % 2
                    if k == 0 and not (isinstance(unit, int) and unit == 0):
                        pe.wait_ge(unit_out, unit * 4 + (b - 3))
                    mm = nc.tensor.matmul(bank[b][:, 0:half], hT[:, lhs0 + k, t * P:(t + 1) * P],
                                          w[:, kk, cb * half:(cb + 1) * half], start=(k == 0), stop=(k == nk - 1))
                    if k == nk - 1 and b < 3:
                        mm.then_inc(unit_bank, 1)
                    if kk == 1 and b == 3:
                        mm.then_inc(w_used, 1)

            def heads_transposed(step, t):
                this = pe.compute_val(step + 1)
                pe.wait_ge(consts, 2)
                pe.wait_ge(staged, this)
                for r in range(GQ):
                    mm = nc.tensor.transpose(bank[6][0:HD, r * P:(r + 1) * P], stage[:, t, r * HD:(r + 1) * HD],
                                             ident[:, :])
                mm.then_inc(qT_bank, 1)

            def scores(step, t, keys):
                pe.wait_ge(qT_out, step + 1)
                nk = P * (t + 1)
                for r in range(GQ):
                    b, o = (4 + r // 2, (r % 2) * SEQ) if t else (4, r * P)
                    mm = nc.tensor.matmul(bank[b][:, o:o + nk], qT[:, r * P:(r + 1) * P], keys[:, 0:nk],
                                          start=True, stop=True)
                mm.then_inc(s_bank, 1)

            pe.wait_ge(consts, 2)
            for n in range(8):
                t, c_ = n // 4, n % 4
                if n % 4 == 0:
                    pe.wait_ge(xhat_ok, t + 1)
                for j in range(4):
                    mm = nc.tensor.transpose(bank[n][:, j * P:(j + 1) * P], chunk_cols(gates[:, t, 0:D], c_, j),
                                             ident[:, :])
                mm.then_inc(xT_bank, 1)
            pe.wait_ge(xT_out, 8)
            pe.wait_ge(ada0_used, CREDIT + KC)
            reduce_to_columns(ada_a, 0, 0)
            pe.wait_ge(ada0_used, CREDIT + 2 * KC)
            reduce_to_columns(ada_b, 0, KC)

            for u in range(2):
                for k in range(KC):
                    if u == 0:
                        pe.wait_ge(h_ready, k + 1)
                    chunk(u, u, k, UW // 2)
            pe.wait_ge(ada_used, CREDIT + KC)
            pe.wait_ge(in_brow, 16)
            reduce_to_rows(ada_a)
            pe.wait_ge(ada_done, 1)
            pe.wait_ge(unit_out, 4)
            for t in range(NT):
                mm = nc.tensor.transpose(bank[6][0:HD, t * P:(t + 1) * P], proj[:, t, KI:KI + HD], ident[:, :])
            mm.then_inc(kT_bank, 1)
            pe.wait_ge(kT_out, 1)

            with pe.Fori(0, 2) as v:
                for s in range(4):
                    t, step, k = s % 2, v * 4 + s, 4 * s
                    chunk(v + 2, v + 2, k, UW // 2, (0, 1))
                    heads_transposed(step, t)
                    chunk(v + 2, v + 2, k, UW // 2, (2, 3))
                    pe.wait_ge(kT_out, 1)
                    pe.wait_ge(relu_out, CREDIT + step)
                    scores(step, t, kT[:, 0, :])
                    for kk in range(k + 1, k + 4):
                        chunk(v + 2, v + 2, kk, UW // 2)

            pe.wait_ge(k_norm, 1)
            pe.wait_ge(relu_out, CREDIT + IDX_STEPS)
            for hk in range(1 + KVH):
                for t in range(NT):
                    o = (hk % 2) * SEQ + t * P
                    mm = nc.tensor.transpose(bank[4 + hk // 2][0:HD, o:o + P], kn[:, t, hk * HD:(hk + 1) * HD],
                                             ident[:, :])
            mm.then_inc(kT_bank, 1)
            pe.wait_ge(ada_used, CREDIT + 2 * KC)
            reduce_to_columns(ada_b, 7, 0)
            pe.wait_ge(ada_done, 2)
            pe.wait_ge(kT_out, 2)

            with pe.Fori(0, N_UNITS_GATE) as u:
                rnd = u + N_UNITS_PROJ
                for s in range(4):
                    t, swa, k = s % 2, s < 2, 4 * s
                    a = u * 4 + s
                    step = u * 4 + (s + IDX_STEPS)
                    chunk(rnd, rnd, k, GW // 2, (0, 1))
                    heads_transposed(step, t)
                    chunk(rnd, rnd, k, GW // 2, (2, 3))
                    pe.wait_ge(kT_out, 2)
                    pe.wait_ge(pT_out, CREDIT + a)
                    keys = kT[:, bass.ds(u + 2, 1), :].rearrange("d a s -> d (a s)") if swa else kT[:, 1, :]
                    scores(step, t, keys)
                    chunk(rnd, rnd, k + 1, GW // 2)
                    chunk(rnd, rnd, k + 2, GW // 2)
                    chunk(rnd, rnd, k + 3, GW // 2, (0, 1))
                    pe.wait_ge(exp_ok, a + 1)
                    for kt in range(t + 1):
                        for r in range(GQ):
                            mm = nc.tensor.transpose(bank[4 + kt][:, r * P:(r + 1) * P],
                                                     scratch[:, r * SEQ + kt * P:r * SEQ + (kt + 1) * P], ident[:, :])
                    mm.then_inc(pT_bank, 1)
                    chunk(rnd, rnd, k + 3, GW // 2, (2, 3))
                    pe.wait_ge(pT_out, CREDIT + a + 1)
                    pe.wait_ge(o_out, CREDIT + a)
                    v_cols = bass.ds(u * HD + VA, HD) if swa else slice(VB, VB + HD)
                    for r in range(GQ):
                        for kt in range(t + 1):
                            o = GQ * SEQ + kt * GQ * P + r * P
                            mm = nc.tensor.matmul(bank[7][:, r * HD:(r + 1) * HD], scratch[:, o:o + P],
                                                  proj[:, kt, v_cols], start=(kt == 0), stop=(kt == t))
                    mm.then_inc(o_bank, 1)

            pe.wait_ge(o_out, CREDIT + ATT_STEPS)
            pe.wait_ge(ada_used, CREDIT + 3 * KC)
            reduce_to_columns(ada_b, 7, 0)

            def transposes(first, source):
                for n in range(8):
                    if first + n >= 3:
                        pe.wait_ge(t_out, first + n - 2)
                    for m in range(4):
                        mm = nc.tensor.transpose(bank[4 + (first + n) % 3][:, m * P:(m + 1) * P], source(n, m),
                                                 ident[:, :])
                    mm.then_inc(t_bank, 1)

            def outputs_of(n, m):
                pair = 4 * (n // 2) + m
                o = QA + pair * P if pair < 8 else QB + (pair - 8) * P
                return proj[:, n % 2, o:o + P]

            transposes(0, outputs_of)
            pe.wait_ge(t_out, 8)
            for rnd in range(2):
                for u in range(2):
                    for k in range(8):
                        chunk(UNITS + rnd, BRANCH0 + 2 * rnd + u, k, GW // 2, slot0=4 * u, lhs0=8 * rnd, nk=8)

            def merged_of(n, m):
                if m == 0:
                    pe.wait_ge(merged, 4 if n < 4 else 8)
                return chunk_cols(gates[:, n % 2, 0:D], n // 2, m)

            transposes(8, merged_of)
            pe.wait_ge(t_out, 16)
            for u in range(2):
                for k in range(KC):
                    chunk(UNITS + 2 + u, OUT0 + u, k, GW // 2)
            pe.wait_ge(ada_used, CREDIT + 4 * KC)
            pe.wait_ge(in_brow, 32)
            pe.wait_ge(ada_done, 3)
            reduce_to_rows(ada_b)

            pe.wait_ge(diag_ok, 1)
            for n in range(8):
                if n >= 4:
                    pe.wait_ge(h2_out, n - 3)
                for j in range(4):
                    mm = nc.tensor.matmul(bank[n % 4][:, j * P:(j + 1) * P], chunk_cols(x1[:, n % 2, :], n // 2, j),
                                          hot_s[:, n % 2, :], start=True, stop=True)
                mm.then_inc(h2_bank, 1)
            pe.wait_ge(h2_out, 8)
            pe.wait_ge(ada_done, 4)
            pe.wait_ge(in_small, SMALL)
            for t in range(NT):
                for k in range(KC):
                    mm = nc.tensor.matmul(bank[4][:, t * 64:t * 64 + NG + NE], hT[:, k, t * P:(t + 1) * P],
                                          w_route[:, k, :], start=(k == 0), stop=(k == KC - 1))
            mm.then_inc(logit_bank, 1)
            pe.wait_ge(onehot_ok, 1)
            pe.wait_ge(consts, 3)
            nc.tensor.matmul(bank[5][:, 0:NG], tri[:, :], onehot[:, 0, :], start=True, stop=True)
            nc.tensor.matmul(bank[5][:, NG:2 * NG], tri[:, :], onehot[:, 1, :], start=True, stop=False)
            nc.tensor.matmul(bank[5][:, NG:2 * NG], ones[:, :], onehot[:, 0, :], start=False, stop=True)
            nc.tensor.matmul(bank[5][:, 2 * NG:3 * NG], ones[:, :], onehot[:, 0, :], start=True, stop=False)
            nc.tensor.matmul(bank[5][:, 2 * NG:3 * NG], ones[:, :], onehot[:, 1, :], start=False, stop=True
                             ).then_inc(rank_bank, 1)

            def gather_rows(n):
                pe.wait_ge(g_hot, n + 1)
                for q in range(4):
                    if q >= 2:
                        pe.wait_ge(g_out, n * 4 + (q - 1))
                    for j in range(4):
                        for t in range(NT):
                            mm = nc.tensor.matmul(bank[7 - q % 2][:, j * P:(j + 1) * P], chunk_cols(x1[:, t, :], q, j),
                                                  hot_s[:, t, :], start=(t == 0), stop=(t == NT - 1))
                    mm.then_inc(g_bank, 1)

            def gate_up(ne):
                pe.wait_ge(e_act, CREDIT + ne)
                for b, s0 in ((4, 0), (5, 4)):
                    for q in range(4):
                        pe.wait_ge(landed[s0 + q], ne * 16 + 16 * (ROUND0 + DENSE_ROUNDS + 1))
                        for j in range(4):
                            mm = nc.tensor.matmul(bank[b][:, :], hG[:, 4 * q + j, :],
                                                  moe_slot(s0 + q)[:, j * FE:(j + 1) * FE],
                                                  start=(q + j == 0), stop=(q + j == 6))
                        mm.then_inc(gu_used, 1)

            def down(ne, first=False, last=False):
                pe.wait_ge(e_act, CREDIT + ne + 1)
                for m in range(4):
                    mm = nc.tensor.transpose(bank[7][:, m * P:(m + 1) * P], act_o[:, m * P:(m + 1) * P], ident[:, :])
                mm.then_inc(e_tr, 1)
                pe.wait_ge(e_trout, ne + 1)
                for m in range(4):
                    pe.wait_ge(landed[RING + m], ne * 16 + 16)
                    for q in range(4):
                        mm = nc.tensor.matmul(bank[q][:, :], actT[:, m * P:(m + 1) * P],
                                              moe_slot(RING + m)[:, q * 512:(q + 1) * 512],
                                              start=(first and m == 0), stop=(last and m == 3))
                        if last and m == 3 and q < 3:
                            mm.then_inc(y_bank, 1)
                    mm.then_inc(d_used, 1)

            def scatter(n):
                pe.wait_ge(y_out, n * 4 + 4)
                for t in range(NT):
                    for q in range(4):
                        if t:
                            pe.wait_ge(sc_out, CREDIT + n * 8 + (q + 1))
                        nc.tensor.matmul(bank[q][:, :], hotT[:, t * P:(t + 1) * P], y_sb[:, q * 512:(q + 1) * 512],
                                         start=True, stop=True).then_inc(sc_bank, 1)

            def group(n, ne, following):
                pe.wait_ge(g_hotT_out, n + 1)
                gate_up(ne)
                gate_up(ne + 1)
                pe.wait_ge(sc_out, CREDIT + n * 8)
                down(ne, first=True)
                with pe.Fori(2, EPG - 1) as e:
                    gate_up(ne + e)
                    down(ne + e - 1)
                gate_up(ne + 7)
                down(ne + 6)
                if following:
                    gather_rows(n + 1)
                    pe.wait_ge(g_out, n * 4 + 7)
                down(ne + 7, last=True)
                scatter(n)

            def moe_pass(ps):
                n0 = ps * NG
                gather_rows(n0)
                gather_routing(n0, 0)
                with pe.Fori(0, NG - 1) as g:
                    group(g + n0, g * EPG + n0 * EPG, True)
                    gather_routing(g + (n0 + 1), g + 1)
                group(n0 + NG - 1, (n0 + NG - 1) * EPG, False)

            def gather_routing(n, g):
                pe.wait_ge(g_out, n * 4 + 4)
                for t in range(NT):
                    nc.tensor.transpose(bank[6][:, t * P:(t + 1) * P], hot[:, t, :], ident[:, :])
                for t in range(NT):
                    mm = nc.tensor.matmul(bank[6][:, SEQ:SEQ + EPG], hot[:, t, :],
                                          comb[:, t, bass.ds(g * EPG, EPG)], start=(t == 0), stop=(t == NT - 1))
                mm.then_inc(g_hotT, 1)

            moe_pass(0)
            pe.wait_ge(route_ok, 1)
            over = pe.value_load(flag[0:1, 0:1], min_val=0, max_val=1)
            with pe.If(over > 0):
                moe_pass(1)

        @block.scalar
        def _(act):
            for credited in (relu_out, pT_out):
                act.sem_inc(credited, CREDIT)

            def take_unit(u, w0, unit, store):
                for b in range(4):
                    if b < 3:
                        act.wait_ge(unit_bank, unit * 3 + (b + 1))
                    else:
                        act.wait_ge(w_used, w0 + RING)
                    store(b, b // 2, b % 2).then_inc(unit_out, 1)

            act.dma_start(cond[:, :].rearrange("p (c j) -> p c j", j=4), c[0].rearrange("(c p j) -> p c j", p=P, j=4)
                          ).then_inc(in_c, 16)
            for t in range(NT):
                act.dma_start(gates[:, t, 0:D], x_v[:, t, :]).then_inc(in_x, 16)
            small = 0

            def load(dst, src):
                act.dma_start(dst, src).then_inc(in_small, 16)
                return 1

            def chunk_col(i):
                return cols[:, i, :].rearrange("p (c j) -> p c j", j=4)

            small += load(chunk_col(C_LN1), ln1_g[0].rearrange("(c p j) -> p c j", p=P, j=4))
            small += load(chunk_col(C_LN2), ln2_g[0].rearrange("(c p j) -> p c j", p=P, j=4))
            for i, s in ((C_BSH1, 0), (C_BSC1, 1), (C_BSH2, 3), (C_BSC2, 4)):
                small += load(chunk_col(i), bias_v[:, s, :, :])
            for i, g in enumerate((swa_q_norm, swa_k_norm, dsa_q_norm, dsa_k_norm)):
                small += load(gain_in[:, i:i + 1], g[0].rearrange("(d a) -> d a", a=1))
            small += load(sinks[:, :], swa_sinks[0:1, :].broadcast_to([P, NH]))
            small += load(b_route[:, 0:NG], b_group[0:1, :].broadcast_to([P, NG]))
            small += load(b_route[:, NG:], b_expert[0:1, :].broadcast_to([P, NE]))
            wr = w_route[:, :, :].rearrange("p (c j) n -> p c j n", j=4)
            for c_ in range(4):
                small += load(wr[:, c_, :, 0:NG], w_group[0].rearrange("(c p j) n -> p c j n", p=P, j=4)[:, c_, :, :]) \
                    if c_ < 2 else 0
            small += load(wr[:, 2, :, 0:NG], w_group[0].rearrange("(c p j) n -> p c j n", p=P, j=4)[:, 2, :, :])
            small += load(wr[:, 3, :, 0:NG], w_group[0].rearrange("(c p j) n -> p c j n", p=P, j=4)[:, 3, :, :])
            for c_ in range(4):
                small += load(wr[:, c_, :, NG:], w_expert[0].rearrange("(c p j) n -> p c j n", p=P, j=4)[:, c_, :, :])
            assert 16 * small == SMALL, small
            act.dma_start(scratch[0:1, 0:D], b_ada[0:1, 2 * D:3 * D]).then_inc(in_brow, 16)

            act.wait_ge(in_c, 16)
            nc.scalar.activation(condr[:, :], cond[:, :], ACT.Exp, scale=-1.0).then_inc(silu_e, 1)
            act.wait_ge(in_x, 32)
            for t in range(NT):
                nc.scalar.activation(proj[:, t, 0:D], gates[:, t, 0:D], ACT.Square, accum_out=stat[:, t:t + 1]
                                     ).then_inc(sq_done, 1)
            for n in range(8):
                t, c_ = n // 4, n % 4
                act.wait_ge(xT_bank, n + 1)
                nc.scalar.activation(hT[:, 4 * c_:4 * c_ + 4, t * P:(t + 1) * P],
                                     bank[n][:, :].rearrange("p (j s) -> p j s", j=4), ACT.Copy).then_inc(xT_out, 1)

            def to_proj(c0, half):
                return lambda b, t, cb: nc.scalar.activation(proj[:, t, bass.ds(c0 + cb * half, half)],
                                                             bank[b][:, 0:half], ACT.Copy)

            for u in range(2):
                take_unit(u, u * RING, u, to_proj(PROJ - UW * (u + 1), UW // 2))

            def take_queries(step):
                act.wait_ge(qT_bank, CREDIT + step + 1)
                nc.scalar.activation(qT[:, :], bank[6][0:HD, :], ACT.Copy).then_inc(qT_out, 1)

            with act.Fori(0, 2) as v:
                for s in range(4):
                    t, step = s % 2, v * 4 + s
                    take_queries(step)
                    act.wait_ge(s_bank, step + 1)
                    act.wait_ge(relu_used, CREDIT + step)
                    dst = scratch[:, t * GQ * SEQ:(t + 1) * GQ * SEQ]
                    if t:
                        nc.scalar.activation(dst[:, 0:512], bank[4][:, :], ACT.Relu, scale=HD ** -0.5)
                        nc.scalar.activation(dst[:, 512:1024], bank[5][:, :], ACT.Relu, scale=HD ** -0.5
                                             ).then_inc(relu_out, 1)
                    else:
                        nc.scalar.activation(dst[:, 0:512], bank[4][:, :], ACT.Relu, scale=HD ** -0.5
                                             ).then_inc(relu_out, 1)
                take_unit(0, v * RING + 2 * RING, v + 2, to_proj(v * (-UW) + (PROJ - 3 * UW), UW // 2))

            with act.Fori(0, N_UNITS_GATE) as u:
                for s in range(4):
                    t, swa, a = s % 2, s < 2, u * 4 + s
                    take_queries(u * 4 + (s + IDX_STEPS))
                    act.wait_ge(max_ok, a + 1)
                    nk = P * (t + 1)
                    for r in range(GQ):
                        p = scratch[:, r * SEQ:r * SEQ + nk]
                        ins = nc.scalar.activation(p, p, ACT.Exp, bias=sm[:, 1, r:r + 1], accum_out=sm[:, 2, r:r + 1])
                    if swa:
                        ins = nc.scalar.activation(sm[:, 4, :], sm[:, 3, :], ACT.Exp)
                    ins.then_inc(exp_ok, 1)
                    act.wait_ge(pT_bank, a + 1)
                    for kt in range(t + 1):
                        o = GQ * SEQ + kt * GQ * P
                        ins = nc.scalar.activation(scratch[:, o:o + GQ * P], bank[4 + kt][:, :], ACT.Copy)
                    ins.then_inc(pT_out, 1)
                take_unit(0, u * RING + N_UNITS_PROJ * RING, u + N_UNITS_PROJ,
                          lambda b, t, cb: nc.scalar.activation(gates[:, t, bass.ds(u * GW + cb * 512, 512)],
                                                                bank[b][:, :], ACT.Exp, scale=-1.0))

            def take_transposes(first):
                for n in range(8):
                    act.wait_ge(t_bank, first + n + 1)
                    k = 4 * (n // 2)
                    nc.scalar.activation(hT[:, k:k + 4, (n % 2) * P:(n % 2 + 1) * P],
                                         bank[4 + (first + n) % 3][:, :].rearrange("p (j s) -> p j s", j=4), ACT.Copy
                                         ).then_inc(t_out, 1)

            act.wait_ge(o_bank, ATT_STEPS)
            act.dma_start(scratch[0:1, 0:D], b_ada[0:1, 5 * D:6 * D]).then_inc(in_brow, 16)
            take_transposes(0)
            for t in range(NT):
                act.dma_start(x1[:, t, :], x_v[:, t, :]).then_inc(in_x1, 16)
            take_transposes(8)
            act.wait_ge(x1_ok, 8)
            for t in range(NT):
                sq = hT[:, t * 8:(t + 1) * 8, :].rearrange("p k s -> p (k s)")
                nc.scalar.activation(sq, x1[:, t, :], ACT.Square, accum_out=stat[:, t:t + 1]).then_inc(sq_done, 1)
            act.wait_ge(r_sub, 1)
            nc.scalar.activation(rt[:, 4, :, 0:NG], rt[:, 3, :, 0:NG], ACT.Exp).then_inc(r_exp, 1)
            act.wait_ge(r_sub, 2)
            nc.scalar.activation(rt[:, 11, :, 0:1], rt[:, 10, :, 0:1], ACT.Exp).then_inc(r_exp, 1)

            def gate_exp(ne):
                act.wait_ge(gu_used, ne * 8 + 4)
                act.wait_ge(e_act, CREDIT + ne)
                nc.scalar.activation(act_e, bank[4][:, :], ACT.Exp, scale=-1.0).then_inc(e_exp, 1)

            def take_act(ne):
                act.wait_ge(e_tr, CREDIT + ne + 1)
                nc.scalar.activation(actT, bank[7][:, :], ACT.Copy).then_inc(e_trout, 1)

            def group(n, ne):
                gate_exp(ne)
                with act.Fori(1, EPG) as e:
                    gate_exp(ne + e)
                    take_act(ne + e - 1)
                take_act(ne + 7)
                for q in range(4):
                    if q < 3:
                        act.wait_ge(y_bank, n * 3 + (q + 1))
                    else:
                        act.wait_ge(d_used, ne * 4 + 4 * EPG)
                    nc.scalar.activation(y_sb[:, q * 512:(q + 1) * 512], bank[q][:, :], ACT.Copy).then_inc(y_out, 1)

            with act.Fori(0, NG) as g:
                group(g, g * EPG)
            act.wait_ge(route_ok, 1)
            over = act.value_load(flag[0:1, 0:1], min_val=0, max_val=1)
            with act.If(over > 0):
                with act.Fori(NG, 2 * NG) as g:
                    group(g, g * EPG)

        @block.vector
        def _(ve):
            for credited in (ada0_used, ada_used, relu_used, o_out, e_act, sc_out):
                ve.sem_inc(credited, CREDIT)
            own = Own(ve, dve_own)
            add, wait = own.add, own.wait
            v_ = nc.vector

            def sum_piece(acc, src, k, used, n):
                ve.wait_ge(used, CREDIT + n)
                v_.scalar_tensor_tensor(out=acc[:, :], in0=src, scalar=cond[:, k], in1=acc[:, :],
                                        op0=ALU.mult, op1=ALU.add).then_inc(used, 1)

            def column(k):
                return bass.ds(k, 1)

            ve.wait_ge(silu_e, 1)
            add(v_.tensor_scalar(condr[:, :], condr[:, :], 1.0, None, ALU.add))
            wait()
            add(v_.reciprocal(condr[:, :], condr[:, :]))
            wait()
            add(v_.tensor_tensor(cond[:, :], cond[:, :], condr[:, :], ALU.mult))

            def mean_squares(done):
                ve.wait_ge(sq_done, done)
                v_.tensor_scalar(stat[:, 2:4], stat[:, 0:2], 1.0 / D, EPS, ALU.mult, ALU.add).then_inc(ms_ok, 1)
                ve.wait_ge(rstd_ok, done // 2)

            mean_squares(2)
            for t in range(NT):
                v_.tensor_scalar(gates[:, t, 0:D], gates[:, t, 0:D], stat[:, 4 + t:5 + t], None, ALU.mult
                                 ).then_inc(xhat_ok, 1)
            wait()
            ve.wait_ge(consts, 2)
            for s, acc in enumerate((ada_a, ada_b)):
                for k in range(KC):
                    ve.wait_ge(landed[k % RING], 16 * (2 * s + k // RING + 1))
                    sum_piece(acc, ring[:, k % RING, :], column(k), ada0_used, s * KC + k)
            ve.wait_ge(in_small, SMALL)
            ve.wait_ge(ada_red, 2)
            add(v_.tensor_tensor(cols[:, C_S1, :], bank[0][:, 0:KC], cols[:, C_BSH1, :], ALU.add))
            add(v_.tensor_tensor(cols[:, C_A1, :], bank[0][:, KC:2 * KC], cols[:, C_BSC1, :], ALU.add))
            wait()
            add(v_.scalar_tensor_tensor(out=cols[:, C_A1, :], in0=cols[:, C_A1, :], scalar=1.0, in1=cols[:, C_LN1, :],
                                        op0=ALU.add, op1=ALU.mult))
            wait()
            ve.wait_ge(xT_out, 8)
            for k in range(KC):
                v_.tensor_scalar(hT[:, k, :], hT[:, k, :], cols[:, C_A1, k:k + 1], cols[:, C_S1, k:k + 1],
                                 ALU.mult, ALU.add).then_inc(h_ready, 1)
            for m in range(2):
                add(v_.tensor_tensor(gain_k[:, m:m + 1], gain_in[:, 2 * m:2 * m + 1], gain_in[:, 2 * m + 1:2 * m + 2],
                                     ALU.mult))
            wait()
            add(v_.tensor_scalar(gain_k[:, :], gain_k[:, :], HD ** -0.5, None, ALU.mult))
            add(v_.memset(ada_a[:, :], 0.0))
            wait()
            with ve.Fori(0, KC // 2) as i:
                for h in range(2):
                    ve.wait_ge(ada_landed[h], i * 16 + 16)
                    sum_piece(ada_a, ada_ring[:, h, :], column(i * 2 + h), ada_used, i * 2 + h)

            def take_rows(acc, red):
                ve.wait_ge(ada_red, red)
                for q in range(4):
                    ins = v_.tensor_copy(acc[:, q * 512:(q + 1) * 512], bank[4 + q][:, :])
                ins.then_inc(ada_done, 1)

            take_rows(ada_a, 3)
            ve.wait_ge(unit_out, 4)
            add(v_.tensor_scalar(wi4[:, :, :], proj[:, :, WI:WI + NH], NH ** -0.5, None, ALU.mult))
            ve.wait_ge(kT_bank, 1)
            v_.tensor_copy(kT[:, 0, :], bank[6][0:HD, 0:SEQ]).then_inc(kT_out, 1)
            add(v_.memset(ada_b[:, :], 0.0))
            ve.wait_ge(consts, 3)
            wait()
            IDX_ADDS = 4 * (GQ - 1)
            with ve.Fori(0, 2) as v:
                own.enter(v, IDX_ADDS)
                for s in range(4):
                    t = s % 2
                    for h in range(2):
                        ve.wait_ge(ada_landed[h], v * 64 + 16 * (KC // 2 + s + 1))
                        sum_piece(ada_b, ada_ring[:, h, :], column(v * 8 + (2 * s + h)), ada_used,
                                  v * 8 + (KC + 2 * s + h))
                    ve.wait_ge(relu_out, CREDIT + v * 4 + (s + 1))
                    nk = P * (t + 1)
                    ve.wait_ge(relu_used, CREDIT + v * 4 + s)
                    for r in range(GQ):
                        src = scratch[:, t * GQ * SEQ + r * nk:t * GQ * SEQ + (r + 1) * nk]
                        ins = v_.scalar_tensor_tensor(out=score[:, t, 0:nk], in0=src,
                                                      scalar=wi4[:, t, bass.ds(v * 8 + (4 * (s // 2) + r), 1)],
                                                      in1=score[:, t, 0:nk], op0=ALU.mult, op1=ALU.add)
                        if r < GQ - 1:
                            add(ins)
                            wait()
                        else:
                            ins.then_inc(relu_used, 1)
                own.leave(2, IDX_ADDS)
            ve.wait_ge(unit_out, 4 * N_UNITS_PROJ)
            ve.wait_ge(relu_used, CREDIT + IDX_STEPS)
            for lo, heads, at in ((QA, NH + KVH, 0), (QB, NH + 1, NH + KVH)):
                for t in range(NT):
                    src = proj[:, t, lo:lo + heads * HD]
                    add(v_.tensor_tensor(scratch[:, 0:heads * HD], src, src, ALU.mult))
                    wait()
                    add(v_.tensor_reduce(qk_rstd[:, t, at:at + heads],
                                         scratch[:, 0:heads * HD].rearrange("p (h d) -> p h d", d=HD), AX, ALU.add))
                    wait()
            v_.tensor_scalar(qk_rstd[:, :, :], qk_rstd[:, :, :], 1.0 / HD, EPS, ALU.mult, ALU.add).then_inc(qk_ms, 1)

            for t in range(NT):
                nk = P * (t + 1)
                add(v_.tensor_tensor(score[:, t, 0:nk], score[:, t, 0:nk], causal[:, SEQ - nk:SEQ], ALU.min))
            wait()
            for t in range(NT):
                nk = P * (t + 1)
                for _ in range(TOPK // 8):
                    add(v_.max(top8[:, :], score[:, t, 0:nk]))
                    wait()
                    add(v_.match_replace(score[:, t, 0:nk], top8[:, :], score[:, t, 0:nk], TAKEN))
                    wait()
                add(v_.tensor_scalar(rel_top[:, t, 0:nk], score[:, t, 0:nk], 0.5 * (TAKEN + NONCAUSAL), FAR,
                                     ALU.is_ge, ALU.mult))
                wait()
                add(v_.tensor_tensor(rel_top[:, t, 0:nk], rel_top[:, t, 0:nk], rel_dsa[:, SEQ - nk:SEQ], ALU.max))

            ve.wait_ge(qk_pow, 1)
            for t in range(NT):
                add(v_.tensor_scalar(kn[:, t, 0:HD], proj[:, t, KB:KB + HD], qk_rstd[:, t, N_RMS - 1:N_RMS], None,
                                     ALU.mult))
                ins = v_.tensor_tensor(kn[:, t, HD:].rearrange("p (h d) -> p h d", d=HD),
                                       proj[:, t, KA:KA + KVH * HD].rearrange("p (h d) -> p h d", d=HD),
                                       qk_rstd[:, t, NH:NH + KVH].unsqueeze(2).broadcast_to([P, KVH, HD]), ALU.mult)
                if t == 0:
                    add(ins)
            ins.then_inc(k_norm, 1)
            ve.wait_ge(ada_red, 4)
            v_.tensor_tensor(cols[:, C_S2, :], bank[7][:, 0:KC], cols[:, C_BSH2, :], ALU.add).then_inc(ada_done, 1)
            ve.wait_ge(kT_bank, 2)
            for hk in range(1 + KVH):
                m = 1 if hk == 0 else 0
                ins = v_.tensor_scalar(kT[:, 1 + hk, :], bank[4 + hk // 2][0:HD, (hk % 2) * SEQ:(hk % 2 + 1) * SEQ],
                                       gain_k[:, m:m + 1], None, ALU.mult)
            ins.then_inc(kT_out, 1)
            add(v_.memset(ada_b[:, :], 0.0))
            wait()

            ATT_ADDS = 4 * (GQ + 1 + 1) + 2 * 3
            with ve.Fori(0, N_UNITS_GATE) as u:
                own.enter(u, ATT_ADDS)
                for s in range(4):
                    t, swa, a = s % 2, s < 2, u * 4 + s
                    nk = P * (t + 1)
                    q0, h0 = (QA, 0) if swa else (QB, NH + KVH)
                    heads = proj[:, t, bass.ds(u * (GQ * HD) + q0, GQ * HD)].rearrange("p (h d) -> p h d", d=HD)
                    ve.wait_ge(qT_bank, CREDIT + u * 4 + (s + IDX_STEPS))
                    v_.tensor_tensor(stage[:, t, :].rearrange("p (h d) -> p h d", d=HD), heads,
                                     qk_rstd[:, t, bass.ds(u * GQ + h0, GQ)].unsqueeze(2).broadcast_to([P, GQ, HD]),
                                     ALU.mult).then_inc(staged, 1)
                    ve.wait_ge(ada_landed[s % 2], u * 32 + 16 * (KC + s // 2 + 1))
                    sum_piece(ada_b, ada_ring[:, s % 2, :], column(u * 4 + s), ada_used, u * 4 + (2 * KC + s))
                    ve.wait_ge(s_bank, u * 4 + (s + IDX_STEPS + 1))
                    for r in range(GQ):
                        b, o = (4 + r // 2, (r % 2) * SEQ) if t else (4, r * P)
                        rel = rel_swa[:, SEQ - nk:SEQ] if swa else rel_top[:, t, 0:nk]
                        add(v_.scalar_tensor_tensor(out=scratch[:, r * SEQ:r * SEQ + nk], in0=rel,
                                                    scalar=nslope[:, bass.ds(u * GQ + ((0 if swa else NH) + r), 1)],
                                                    in1=bank[b][:, o:o + nk], op0=ALU.mult, op1=ALU.add))
                    wait()
                    p = scratch[:, 0:GQ * SEQ].rearrange("p (r s) -> p r s", r=GQ)[:, :, 0:nk]
                    add(v_.tensor_reduce(sm[:, 0, :], p, AX, ALU.max))
                    wait()
                    if swa:
                        sink = sinks[:, bass.ds(u * GQ, GQ)]
                        add(v_.tensor_tensor(sm[:, 0, :], sm[:, 0, :], sink, ALU.max))
                        wait()
                        add(v_.tensor_tensor(sm[:, 3, :], sink, sm[:, 0, :], ALU.subtract))
                    v_.tensor_scalar(sm[:, 1, :], sm[:, 0, :], -1.0, None, ALU.mult).then_inc(max_ok, 1)
                    ve.wait_ge(exp_ok, a + 1)
                    if swa:
                        add(v_.tensor_tensor(sm[:, 5, :], sm[:, 2, :], sm[:, 4, :], ALU.add))
                        wait()
                    add(v_.reciprocal(sm[:, 6, :], sm[:, 5 if swa else 2, :]))
                    wait()
                    ve.wait_ge(o_bank, a + 1)
                    v_.tensor_tensor(heads, bank[7][:, 0:GQ * HD].rearrange("p (h d) -> p h d", d=HD),
                                     sm[:, 6, :].unsqueeze(2).broadcast_to([P, GQ, HD]), ALU.mult).then_inc(o_out, 1)
                own.leave(N_UNITS_GATE, ATT_ADDS)
            ve.wait_ge(ada_red, 5)
            add(v_.tensor_tensor(cols[:, C_A2, :], bank[7][:, 0:KC], cols[:, C_BSC2, :], ALU.add))
            wait()
            v_.scalar_tensor_tensor(out=cols[:, C_A2, :], in0=cols[:, C_A2, :], scalar=1.0, in1=cols[:, C_LN2, :],
                                    op0=ALU.add, op1=ALU.mult).then_inc(ada_done, 1)
            add(v_.memset(ada_b[:, :], 0.0))
            wait()

            def gt2_piece(k):
                ve.wait_ge(ada_landed[k % 2], 16 * (KC + KC // 2 + k // 2 + 1))
                sum_piece(ada_b, ada_ring[:, k % 2, :], column(k), ada_used, 3 * KC + k)

            def unit_complete(b, unit, w_after):
                if b < 3:
                    ve.wait_ge(unit_bank, 3 * unit + b + 1)
                else:
                    ve.wait_ge(w_used, w_after)

            ve.wait_ge(unit_out, 4 * UNITS)
            for rnd in range(2):
                for u in range(2):
                    nu = 2 * rnd + u
                    for b in range(4):
                        t, c0 = b // 2, u * GW + (b % 2) * 512
                        g = gates[:, t, rnd * D + c0:rnd * D + c0 + 512]
                        add(v_.tensor_scalar(g, g, 1.0, None, ALU.add))
                        wait()
                        add(v_.reciprocal(g, g))
                        wait()
                        unit_complete(b, BRANCH0 + nu, UNITS * RING + 4 * (nu + 1))
                        v_.tensor_tensor(g, g, bank[b][:, :], ALU.mult).then_inc(unit_out, 1)
                        if rnd:
                            ve.wait_ge(unit_out, 4 * (BRANCH0 + nu) + b + 1)
                            ga = gates[:, t, c0:c0 + 512]
                            v_.tensor_tensor(ga, ga, g, ALU.add).then_inc(merged, 1)
                        if b % 2:
                            gt2_piece(2 * nu + b // 2)
            ve.wait_ge(in_x1, 32)
            ve.wait_ge(ada_done, 1)
            for u in range(2):
                for b in range(4):
                    gt2_piece(8 + 4 * u + b)
                for b in range(4):
                    t, c0 = b // 2, u * GW + (b % 2) * 512
                    unit_complete(b, OUT0 + u, (UNITS + 2 + u + 1) * RING)
                    if u + b:
                        ve.wait_ge(x1_ok, 4 * u + b)
                    v_.tensor_tensor(tmp, bank[b][:, :], ada_a[:, c0:c0 + 512], ALU.mult).then_inc(unit_out, 1)
                    ve.wait_ge(unit_out, 4 * (OUT0 + u) + b + 1)
                    v_.tensor_tensor(x1[:, t, c0:c0 + 512], x1[:, t, c0:c0 + 512], tmp, ALU.add).then_inc(x1_ok, 1)
            mean_squares(4)
            for t in range(NT):
                ins = v_.tensor_scalar(hot_s[:, t, :], ident[:, :], stat[:, 4 + t:5 + t], None, ALU.mult)
            ins.then_inc(diag_ok, 1)
            take_rows(ada_b, 6)
            ve.wait_ge(ada_done, 4)

            def take_scaled(dst, b, c_, done):
                for j in range(4):
                    k = 4 * c_ + j
                    ins = v_.tensor_scalar(dst(k), bank[b][:, j * P:(j + 1) * P], cols[:, C_A2, k:k + 1],
                                           cols[:, C_S2, k:k + 1], ALU.mult, ALU.add)
                ins.then_inc(done, 1)

            for n in range(8):
                ve.wait_ge(h2_bank, n + 1)
                take_scaled(lambda k: hT[:, k, (n % 2) * P:(n % 2 + 1) * P], n % 4, n // 2, h2_out)

            def r(i, w=8):
                return rt[:, i, :, 0:w]

            def wide(v, w):
                return v.broadcast_to([P, NT, w])

            def row(v, w):
                return v[:, 0:w].unsqueeze(1).broadcast_to([P, NT, w])

            def do(ins):
                add(ins)
                wait()

            def first_max(src, w, m, key, km, hot_out):
                do(v_.tensor_reduce(m, src, AX, ALU.max))
                do(v_.tensor_tensor(key, src, wide(m, w), ALU.is_equal))
                do(v_.tensor_tensor(key, key, row(firstw, w), ALU.mult))
                do(v_.tensor_reduce(km, key, AX, ALU.max))
                return v_.tensor_tensor(hot_out, key, wide(km, w), ALU.is_equal)

            ve.wait_ge(logit_bank, 1)
            do(v_.tensor_tensor(lg[:, :, :], bank[4][:, 0:2 * 64].rearrange("p (t n) -> p t n", t=NT)[:, :, 0:NG + NE],
                                row(b_route, NG + NE), ALU.add))
            gl = lg[:, :, 0:NG]
            first_max(gl, NG, r(0, 1), r(1, NG), r(2, 1), onehot[:, :, :]).then_inc(onehot_ok, 1)
            v_.tensor_tensor(r(3, NG), gl, wide(r(0, 1), NG), ALU.subtract).then_inc(r_sub, 1)
            ve.wait_ge(onehot_ok, 1)
            for t in range(NT):
                add(v_.tensor_tensor(esel[:, t, :].rearrange("p (g e) -> p g e", g=NG),
                                     lg[:, t, NG:].rearrange("p (g e) -> p g e", g=NG),
                                     onehot[:, t, :].unsqueeze(2).broadcast_to([P, NG, EPG]), ALU.mult))
            wait()
            for t in range(NT):
                add(v_.tensor_reduce(rt[:, 5, t, :], esel[:, t, :].rearrange("p (g e) -> p e g", g=NG), AX, ALU.add))
            wait()
            es = r(5)
            do(first_max(es, EPG, r(6, 1), r(7), r(2, 1), r(8)))
            do(v_.scalar_tensor_tensor(out=r(7), in0=r(8), scalar=-3.0e38, in1=es, op0=ALU.mult, op1=ALU.add))
            do(first_max(r(7), EPG, r(9, 1), r(12), r(2, 1), r(13)))
            v_.tensor_tensor(r(10, 1), r(9, 1), r(6, 1), ALU.subtract).then_inc(r_sub, 1)
            ve.wait_ge(r_exp, 2)
            do(v_.tensor_reduce(r(14, 1), r(4, NG), AX, ALU.add))
            do(v_.tensor_scalar(r(15, 1), r(11, 1), 1.0, None, ALU.add))
            do(v_.tensor_tensor(r(14, 1), r(14, 1), r(15, 1), ALU.mult))
            do(v_.reciprocal(r(14, 1), r(14, 1)))
            do(v_.tensor_tensor(r(15, 1), r(14, 1), r(11, 1), ALU.mult))
            do(v_.tensor_tensor(r(8), r(8), wide(r(14, 1), 8), ALU.mult))
            do(v_.tensor_tensor(r(13), r(13), wide(r(15, 1), 8), ALU.mult))
            do(v_.tensor_tensor(r(8), r(8), r(13), ALU.add))
            for t in range(NT):
                add(v_.tensor_tensor(comb[:, t, :].rearrange("p (g e) -> p g e", g=NG),
                                     onehot[:, t, :].unsqueeze(2).broadcast_to([P, NG, EPG]),
                                     rt[:, 8, t, :].unsqueeze(1).broadcast_to([P, NG, EPG]), ALU.mult))
            ve.wait_ge(rank_bank, 1)
            do(v_.tensor_tensor(rank[:, :, :], bank[5][:, 0:NT * NG].rearrange("p (t g) -> p t g", t=NT),
                                onehot[:, :, :], ALU.mult))
            do(v_.tensor_scalar(rank[:, :, :], rank[:, :, :], -1.0, None, ALU.add))
            do(v_.tensor_reduce(cnt[:, :], bank[5][:, NT * NG:(NT + 1) * NG], AX, ALU.max))
            v_.tensor_scalar(flag[:, :], cnt[:, :], float(P), None, ALU.is_gt).then_inc(route_ok, 1)

            def one_hots(g):
                for t in range(NT):
                    rk = rank[:, t, bass.ds(g, 1)]
                    add(v_.tensor_scalar(hot[:, t, :], iota[:, :], rk, None, ALU.is_equal))
                    ins = v_.tensor_scalar(hot_s[:, t, :], iota[:, :], rk, stat[:, 4 + t:5 + t], ALU.is_equal, ALU.mult)
                    if t == 0:
                        add(ins)
                ins.then_inc(g_hot, 1)

            HOT_ADDS = 3

            def take_rows_gathered(n):
                for q in range(4):
                    ve.wait_ge(g_bank, n * 4 + (q + 1))
                    take_scaled(lambda k: hG[:, k, :], 7 - q % 2, q, g_out)

            def take_routing(n):
                ve.wait_ge(g_hotT, n + 1)
                v_.tensor_copy(hotT, bank[6][:, 0:SEQ])
                v_.tensor_copy(comb_s, bank[6][:, SEQ:SEQ + EPG]).then_inc(g_hotT_out, 1)

            def expert(e, ne):
                ve.wait_ge(e_exp, ne + 1)
                do(v_.tensor_scalar(act_t, act_e, 1.0, None, ALU.add))
                do(v_.reciprocal(act_t, act_t))
                do(v_.tensor_tensor(act_t, act_t, bank[4][:, :], ALU.mult))
                ve.wait_ge(gu_used, ne * 8 + 8)
                ve.wait_ge(e_tr, CREDIT + ne)
                v_.scalar_tensor_tensor(out=act_o, in0=bank[5][:, :], scalar=comb_s[:, bass.ds(e, 1)], in1=act_t,
                                        op0=ALU.mult, op1=ALU.mult).then_inc(e_act, 1)

            def take_scatter(n):
                for t in range(NT):
                    for q in range(4):
                        ve.wait_ge(sc_bank, n * 8 + (4 * t + q + 1))
                        if t + q:
                            ve.wait_ge(sc_out, CREDIT + n * 8 + (4 * t + q))
                        do(v_.tensor_tensor(tmp, bank[q][:, :], gt2[:, q * 512:(q + 1) * 512], ALU.mult))
                        xs = x1[:, t, q * 512:(q + 1) * 512]
                        v_.tensor_tensor(xs, xs, tmp, ALU.add).then_inc(sc_out, 1)

            def group(g, n, ne, following):
                ve.wait_ge(g_hotT_out, n + 1)
                if following:
                    one_hots(g + 1)
                own_before = own.n
                outer = (own.start, own.n)
                with ve.Fori(0, EPG) as e:
                    own.start, own.n = outer[0] + outer[1] + e * 3, 0
                    expert(e, ne + e)
                    assert own.n == 3
                own.start, own.n = outer[0], outer[1] + EPG * 3
                if following:
                    take_rows_gathered(n + 1)
                take_scatter(n)
                if following:
                    take_routing(n + 1)

            GROUP_ADDS = HOT_ADDS + 3 * EPG + 8

            def moe_pass(ps):
                n0 = ps * NG
                if ps:
                    do(v_.tensor_scalar(rank[:, :, :], rank[:, :, :], -float(P), None, ALU.add))
                one_hots(0)
                take_rows_gathered(n0)
                take_routing(n0)
                with ve.Fori(0, NG - 1) as g:
                    own.enter(g, GROUP_ADDS)
                    saved = own.outer
                    group(g, g + n0, g * EPG + n0 * EPG, True)
                    own.outer = saved
                    own.leave(NG - 1, GROUP_ADDS)
                group(NG - 1, n0 + NG - 1, (n0 + NG - 1) * EPG, False)

            moe_pass(0)
            ve.wait_ge(route_ok, 1)
            over = ve.value_load(flag[0:1, 0:1], min_val=0, max_val=1)
            with ve.If(over > 0):
                moe_pass(1)


_INS = ["x", "c", "w_ada", "b_ada", "ln1_g", "w_in", "swa_q_norm", "swa_k_norm", "swa_sinks", "dsa_q_norm",
        "dsa_k_norm", "w_branch_a", "w_branch_b", "w_out", "ln2_g", "w_group", "b_group", "w_expert", "b_expert",
        "w_gate_up", "w_up", "w_down"]


def kernel(**inputs):
    import concourse.bacc as bacc
    from concourse.bass_utils import run_bass_kernel_spmd

    nc = bacc.Bacc("TRN2", target_bir_lowering=False, num_devices=1)
    arrays, args = {}, []
    for name in _INS:
        a = np.ascontiguousarray(inputs[name])
        arrays[f"in_{name}"] = a
        args.append(nc.dram_tensor(f"in_{name}", a.shape, mybir.dt.from_np(a.dtype), kind="ExternalInput").ap())
    args.append(nc.dram_tensor("out_x", (1, SEQ, D), F32, kind="ExternalOutput").ap())
    decoder_block(nc, *args)
    r = run_bass_kernel_spmd(nc, [arrays], core_ids=[0])
    return r.results[0]["out_x"]
```

```python
from contextlib import ExitStack


import numpy as np
import concourse.bass as bass
from concourse import mybir

F32 = mybir.dt.float32
F32R = mybir.dt.float32r
I32 = mybir.dt.int32
ALU = mybir.AluOpType
ACT = mybir.ActivationFunctionType
AX = mybir.AxisListType.X

P = 128
D = 2048
SEQ = 256
NT = SEQ // P
HD = 64
NH = 16
KVH = 4
GQ = 4
TOPK = min(256, SEQ // 4)
KC = D // P
NC4 = KC // 4
QA, KA, VA = 0, 1024, 1280
QB, KB, VB = 1536, 2560, 2624
QI, KI, WI = 2688, 3712, 3776
PROJ = 3792
IN_W = PROJ + 2 * D
UW = PROJ // 4
GW = 1024
N_UNITS_PROJ = PROJ // UW
N_UNITS_GATE = 2 * D // GW
RING = 4
SLOT = 2048
HALF = SLOT // 2
NSPLIT = 4
NG, EPG = 4, 8
NE = NG * EPG
FE = 512
EPS = 1e-6
FAR = 1.0e32
NONCAUSAL = -3.0e38
TAKEN = -3.3e38



def slope(i):
    return 2.0 ** (-8.0 * (i + 1) / (2 * NH))


def decoder_block(nc, x, c, w_ada, b_ada, ln1_g, w_in, swa_q_norm, swa_k_norm, swa_sinks,
                  dsa_q_norm, dsa_k_norm, w_branch_a, w_branch_b, w_out, ln2_g, w_group, b_group,
                  w_expert, b_expert, w_gate_up, w_up, w_down, out):
    x_v = x[0].rearrange("(t p) d -> p t d", p=P)
    out_v = out[0].rearrange("(t p) d -> p t d", p=P)
    ada_v = w_ada[0].rearrange("(c p j) n -> p c j n", p=P, j=4)
    in_v = w_in[0].rearrange("(c p j) n -> p c j n", p=P, j=4)
    branch_v = [w[0].rearrange("(k p) n -> p k n", p=P) for w in (w_branch_a, w_branch_b)]
    wo_v = w_out[0].rearrange("(c p j) n -> p c j n", p=P, j=4)
    gate_v = w_gate_up[0].rearrange("g e (c p j) f -> p (g e) c j f", p=P, j=4)
    up_v = w_up[0].rearrange("g e (c p j) f -> p (g e) c j f", p=P, j=4)
    down_v = w_down[0].rearrange("g e (k p) d -> p (g e) k d", p=P)
    bias_v = b_ada[0].rearrange("(s c p j) -> p s c j", s=6, p=P, j=4)

    ctx = ExitStack()
    with ctx:
        def sb(name, shape, dt=F32):
            return ctx.enter_context(nc.sbuf_tensor(name, shape, dt))

        def sem(name):
            return ctx.enter_context(nc.semaphore(name))

        sizes = dict(ring=RING * SLOT, split=2 * NSPLIT * HALF, ada_ring=2 * HALF, hT=2 * KC * SEQ, proj=NT * PROJ,
                     gates=NT * 2 * D, ada_a=D, ada_b=D)
        at, total = {}, 0
        for name, size in sizes.items():
            at[name], total = total, total + size
        arena_byte = -(-nc.sbuf_base // 32) * 32
        arena = nc.alloc_sbuf_tensor("arena", [P, total], F32)

        def part(offset, size):
            return arena[:, offset:offset + size]

        def f32r(name, offset, shape):
            return nc.alloc_sbuf_tensor_at(name, shape, F32R, offset=arena_byte + 4 * offset)

        ring = part(at["ring"], RING * SLOT).rearrange("p (i n) -> p i n", i=RING)
        w_hi = f32r("w_hi", at["split"], [P, NSPLIT, HALF])
        w_lo = f32r("w_lo", at["split"] + NSPLIT * HALF, [P, NSPLIT, HALF])
        ada_ring = part(at["ada_ring"], 2 * HALF).rearrange("p (i n) -> p i n", i=2)
        hT_hi = f32r("hT_hi", at["hT"], [P, KC, SEQ])
        hT_lo = f32r("hT_lo", at["hT"] + KC * SEQ, [P, KC, SEQ])
        proj = part(at["proj"], NT * PROJ).rearrange("p (t n) -> p t n", t=NT)
        gates = part(at["gates"], NT * 2 * D).rearrange("p (t n) -> p t n", t=NT)
        x_raw = gates[:, :, 0:D]
        xT_raw = gates[:, :, D:2 * D].rearrange("p t (k s) -> p t k s", k=KC)
        relu_s = gates[:, :, 0:GQ * SEQ]
        squares = gates[:, 0, 0:(NH + KVH) * HD]
        brow1 = gates[0:1, 1, D:2 * D]
        ada_a = part(at["ada_a"], D)
        ada_b = part(at["ada_b"], D)
        prob, probT = proj[:, 0, QI:QI + GQ * SEQ], proj[:, 1, QI:QI + GQ * SEQ]
        stage = sb("stage", [P, 2, GQ * HD])
        qT_full = sb("qT", [P, GQ * P])
        kT_full = sb("kT", [P, 2 + KVH, SEQ])
        qT = qT_full[0:HD, :]
        kT = kT_full[0:HD, :, :]
        ident = sb("ident", [P, P])
        ones = sb("ones", [P, P])
        tri = sb("tri", [P, P])
        iota = sb("iota", [P, P])
        rel_swa = sb("rel_swa", [P, SEQ])
        rel_dsa = sb("rel_dsa", [P, SEQ])
        causal = sb("causal", [P, SEQ])
        rel_top = sb("rel_top", [P, NT, SEQ])
        score = sb("score", [P, NT, SEQ])
        top8 = sb("top8", [P, 8])
        nslope = sb("nslope", [P, 2 * NH])
        sinks = sb("sinks", [P, NH])
        wi4 = sb("wi4", [P, NT, NH])
        condr = sb("condr", [P, KC])
        cond = sb("cond", [P, KC])
        cols = sb("cols", [P, 10, KC])
        (C_LN1, C_BSH1, C_BSC1, C_LN2, C_BSH2, C_BSC2, C_A1, C_S1, C_A2, C_S2) = range(10)
        gain_in = sb("gain_in", [HD, 4])
        gain_k = sb("gain_k", [HD, 2])
        stat = sb("stat", [P, 6])
        N_RMS = 2 * NH + KVH + 1
        mhalf = sb("mhalf", [P, 1])
        qk_rstd = sb("qk_rstd", [P, NT, N_RMS])
        kn = sb("kn", [P, NT, (1 + KVH) * HD])
        sm = sb("sm", [P, 7, GQ])
        w_route = sb("w_route", [P, KC, NG + NE])
        b_route = sb("b_route", [P, NG + NE])
        firstw = sb("firstw", [P, 8])
        rt = rel_top[:, :, :].rearrange("p t (i e) -> p (t i) e", e=NT * 8)[:, 0:16, :].rearrange(
            "p i (t e) -> p i t e", t=NT)
        lg = score[:, 0, 0:NT * (NG + NE)].rearrange("p (t n) -> p t n", t=NT)
        esel = score[:, 1, 0:NT * NE].rearrange("p (t n) -> p t n", t=NT)
        onehot = sb("onehot", [P, NT, NG])
        comb = sb("comb", [P, NT, NE])
        rank = sb("rank", [P, NT, NG])
        cnt = sb("cnt", [P, 1])
        flag = sb("flag", [P, 1], I32)
        x1 = part(at["proj"], NT * D).rearrange("p (t d) -> p t d", t=NT)
        tail = at["proj"] + NT * D
        brow2 = arena[0:1, tail:tail + D]
        hot_at = tail + SLOT
        hot_s = part(hot_at, 2 * P).rearrange("p (t s) -> p t s", t=NT)
        hot = part(hot_at + 2 * P, 2 * P).rearrange("p (t s) -> p t s", t=NT)
        hotT = part(hot_at + 4 * P, SEQ)
        comb_s = part(hot_at + 4 * P + SEQ, EPG)
        h2T = part(at["hT"] + KC * SEQ, KC * SEQ).rearrange("p (k s) -> p k s", k=KC)
        hG_hi = f32r("hG_hi", at["hT"], [P, KC, P])
        hG_lo = f32r("hG_lo", at["hT"] + KC * P, [P, KC, P])
        y_sb = ada_a
        gt2 = ada_b
        act_e, act_t, act_o = (kT_full[:, 2 * i:2 * i + 2, :].rearrange("p a b -> p (a b)") for i in range(3))
        actT = qT_full[:, :]
        tmp = stage[:, :, :].rearrange("p a b -> p (a b)")
        gate_slot = part(at["gates"], 4 * SLOT).rearrange("p (i n) -> p i n", i=4)
        up_slot = ring
        down_slot = [part(o, SLOT) for o in (tail, at["ada_ring"], at["hT"] + KC * SEQ, at["hT"] + KC * SEQ + SLOT)]

        bank = [ctx.enter_context(nc.psum_tensor(f"bank{i}", [P, 512], F32)) for i in range(8)]

        in_c, in_x, in_small, in_brow, in_x1, stored = map(
            sem, ("in_c", "in_x", "in_small", "in_brow", "in_x1", "stored"))
        landed = [sem(f"landed{i}") for i in range(RING)]
        gate_landed = [sem(f"gate_landed{i}") for i in range(4)]
        down_landed = [sem(f"down_landed{i}") for i in range(4)]
        ada_landed = [sem("ada_landed0"), sem("ada_landed1")]
        consts, rstd_ok, qk_pow, staged = map(sem, ("consts", "rstd_ok", "qk_pow", "staged"))
        ada0_used, ada_used, ada_red, ada_done = map(sem, ("ada0_used", "ada_used", "ada_red", "ada_done"))
        hi_ok, split_ok, split_used = map(sem, ("hi_ok", "split_ok", "split_used"))
        unit_bank, unit_out = map(sem, ("unit_bank", "unit_out"))
        silu_e, sq_done, ms_ok, xhat_ok, xT_bank, xT_out, h_raw, h_hi, h_ready = map(
            sem, ("silu_e", "sq_done", "ms_ok", "xhat_ok", "xT_bank", "xT_out", "h_raw", "h_hi", "h_ready"))
        kT_bank, kT_out, k_norm, qk_ms, qT_bank, qT_out = map(
            sem, ("kT_bank", "kT_out", "k_norm", "qk_ms", "qT_bank", "qT_out"))
        s_bank, relu_out, relu_used, max_ok, exp_ok = map(
            sem, ("s_bank", "relu_out", "relu_used", "max_ok", "exp_ok"))
        pT_bank, pT_out, o_bank, o_out = map(sem, ("pT_bank", "pT_out", "o_bank", "o_out"))
        t_bank, t_hi, t_out, gate_sum, merged, x1_ok = map(
            sem, ("t_bank", "t_hi", "t_out", "gate_sum", "merged", "x1_ok"))
        diag_ok, h2_bank, h2_out, logit_bank, r_sub, r_exp, onehot_ok, rank_bank, route_ok = map(
            sem, ("diag_ok", "h2_bank", "h2_out", "logit_bank", "r_sub", "r_exp", "onehot_ok", "rank_bank",
                  "route_ok"))
        g_hot, g_bank, g_out, g_hotT, g_hotT_out = map(
            sem, ("g_hot", "g_bank", "g_out", "g_hotT", "g_hotT_out"))
        d_used, e_exp, e_act, e_tr, e_trout = map(sem, ("d_used", "e_exp", "e_act", "e_tr", "e_trout"))
        y_bank, y_out, sc_bank, sc_out = map(sem, ("y_bank", "y_out", "sc_bank", "sc_out"))
        dve_own, act_own, pool_own = map(sem, ("dve_own", "act_own", "pool_own"))

        block = ctx.enter_context(nc.Block())
        CREDIT = 1
        ROUND0 = 2 * KC // RING
        UNITS = N_UNITS_PROJ + N_UNITS_GATE
        K_GATE, K_BRANCH = KC * N_UNITS_PROJ, KC * UNITS
        K_OUT = K_BRANCH + 4 * 8
        K_MOE = K_OUT + 2 * KC
        LEAD = 3
        ADA_SECTION = 2 * KC
        BRANCH0 = UNITS
        OUT0 = BRANCH0 + 4
        IDX_STEPS = 2 * NT * 2
        ATT_STEPS = 2 * NT * (NH // GQ)
        SMALL = 16 * 21

        class Own:

            def __init__(self, eng, own_sem):
                self.eng, self.sem, self.start, self.n = eng, own_sem, 0, 0

            def add(self, ins):
                ins.then_inc(self.sem, 1)
                self.n += 1

            def wait(self):
                self.eng.wait_ge(self.sem, self.start + self.n)

            def enter(self, i, each):
                self.outer = (self.start, self.n)
                self.start, self.n = self.start + self.n + i * each, 0

            def leave(self, times, each):
                assert self.n == each, (self.n, each)
                start, n = self.outer
                self.start, self.n = start, n + times * each


        def chunk_cols(v, c_, j):
            return v[:, 512 * c_:512 * c_ + 512].rearrange("p (q j) -> p j q", j=4)[:, j, :]

        def one(i):
            return bass.ds(i, 1)

        def dense_half(i):
            return ring[:, (i // 2) % RING, (i % 2) * HALF:(i % 2 + 1) * HALF]

        def moe_half(h):
            slots = gate_slot if h < 8 else up_slot
            return slots[:, (h % 8) // 2, (h % 2) * HALF:(h % 2 + 1) * HALF]

        @block.sync
        def _(sp):
            def pair(i, width):
                return ring[:, i, :].rearrange("p (j n) -> p j n", j=2)[:, :, 0:width]

            def split_before(m):
                sp.wait_ge(split_ok, 2 * (m - RING) + 2)

            for n in range(2 * KC):
                if n >= RING:
                    sp.wait_ge(ada0_used, CREDIT + n - RING + 1)
                k = n % KC
                sp.dma_start(ring[:, n % RING, :], ada_v[:, k // 4, k % 4, (n // KC) * D:(n // KC + 1) * D]
                             ).then_inc(landed[n % RING], 16)
            for u in range(N_UNITS_PROJ):
                c0 = PROJ - UW * (u + 1)
                for i in range(8):
                    m = 8 * u + i
                    if m < RING:
                        sp.wait_ge(ada0_used, CREDIT + 2 * KC - RING + m + 1)
                    else:
                        split_before(m)
                    sp.dma_start(pair(m % RING, UW), in_v[:, i // 2, 2 * (i % 2):2 * (i % 2) + 2, c0:c0 + UW]
                                 ).then_inc(landed[m % RING], 16)
            with sp.Fori(0, N_UNITS_GATE) as u:
                for i in range(8):
                    sp.wait_ge(split_ok, u * KC + (K_GATE + 2 * (i - RING) + 2))
                    sp.dma_start(pair(i % RING, GW),
                                 in_v[:, i // 2, 2 * (i % 2):2 * (i % 2) + 2, bass.ds(u * GW + PROJ, GW)]
                                 ).then_inc(landed[i % RING], 16)
            for nu in range(4):
                for i in range(4):
                    split_before(K_BRANCH // 2 + 4 * nu + i)
                    sp.dma_start(pair(i, GW), branch_v[nu // 2][:, 2 * i:2 * i + 2, (nu % 2) * GW:(nu % 2 + 1) * GW]
                                 ).then_inc(landed[i], 16)
            for u in range(2):
                for i in range(8):
                    split_before(K_OUT // 2 + 8 * u + i)
                    sp.dma_start(pair(i % RING, GW),
                                 wo_v[:, i // 2, 2 * (i % 2):2 * (i % 2) + 2, u * GW:(u + 1) * GW]
                                 ).then_inc(landed[i % RING], 16)

            def gate_up_pieces(e, ne, first=False):
                for q in range(8):
                    slots, signals, view = (gate_slot, gate_landed, gate_v) if q < 4 else (up_slot, landed, up_v)
                    if first and q < 4:
                        if q == 0:
                            sp.wait_ge(t_bank, 16)
                    else:
                        sp.wait_ge(split_ok, (K_MOE - 2 * RING + 2 * (q - 4) + 2) if first
                                   else (ne * 16 + (K_MOE - 16 + 2 * q + 2)))
                    sp.dma_start(slots[:, q % 4, :].rearrange("p (j f) -> p j f", j=4),
                                 view[:, one(e), q % 4, :, :].rearrange("p a j f -> p (a j) f")
                                 ).then_inc(signals[q % 4], 16)

            def down_pieces(e, ne, first=False):
                for m in range(4):
                    if not first:
                        sp.wait_ge(d_used, ne * 4 + (m - 3))
                    elif m == 0:
                        sp.wait_ge(ada_red, 6)
                    elif m == 2:
                        sp.wait_ge(logit_bank, 1)
                    sp.dma_start(down_slot[m], down_v[:, one(e), m, :].rearrange("p a d -> p (a d)")
                                 ).then_inc(down_landed[m], 16)

            gate_up_pieces(0, 0, first=True)
            down_pieces(0, 0, first=True)
            gate_up_pieces(1, 1)
            with sp.Fori(1, NE - 1) as e:
                gate_up_pieces(e + 1, e + 1)
                down_pieces(e, e)
            down_pieces(NE - 1, NE - 1)

            sp.wait_ge(route_ok, 1)
            over = sp.value_load(flag[0:1, 0:1], min_val=0, max_val=1)
            with sp.If(over > 0):
                gate_up_pieces(0, NE)
                with sp.Fori(0, NE - 1) as e:
                    gate_up_pieces(e + 1, e + (NE + 1))
                    down_pieces(e, e + NE)
                down_pieces(NE - 1, 2 * NE - 1)
                sp.wait_ge(sc_out, CREDIT + 2 * 8 * NG)
                sp.nop()
            sp.wait_ge(sc_out, CREDIT + 8 * NG)
            for t in range(NT):
                sp.dma_start(out_v[:, t, :], x1[:, t, :]).then_inc(stored, 16)
            sp.wait_ge(stored, 16 * NT)

        @block.gpsimd
        def _(pool):
            own = Own(pool, pool_own)

            def link(ins):
                own.add(ins)
                own.wait()

            def ada_piece(section, c_, j, h, before):
                if before is not None:
                    pool.wait_ge(ada_used, before)
                o = section * D + h * HALF
                nc.gpsimd.dma_start(ada_ring[:, h, :], ada_v[:, one(c_), j, o:o + HALF].rearrange("p a n -> p (a n)")
                                    ).then_inc(ada_landed[h], 16)

            def ada_section(i, c0=0):
                with pool.Fori(c0, NC4) as c_:
                    for j in range(4):
                        for h in range(2):
                            ada_piece(2 + i, c_, j, h, c_ * 8 + (CREDIT + ADA_SECTION * i + 2 * j + h - 1))

            link(nc.gpsimd.memset(ident[:, :], 0.0))
            nc.gpsimd.memset(ada_a[:, :], 0.0)
            nc.gpsimd.memset(ada_b[:, :], 0.0)
            nc.gpsimd.affine_select(out=ident[:, :], in_=ident[:, :], compare_op=ALU.not_equal, fill=1.0, base=0,
                                    pattern=[[-1, P]], channel_multiplier=1).then_inc(consts, 1)
            nc.gpsimd.memset(ones[:, :], 1.0).then_inc(consts, 1)
            link(nc.gpsimd.memset(mhalf[:, :], -0.5))

            def power(v, n, done):
                nc.gpsimd.tensor_tensor(v, v, mhalf[:, 0:1].broadcast_to([P, n]), ALU.pow).then_inc(done, 1)

            pool.wait_ge(ms_ok, 1)
            nc.gpsimd.tensor_tensor(stat[:, 4:6], stat[:, 2:4], mhalf[:, 0:1].broadcast_to([P, NT]), ALU.pow
                                    ).then_inc(rstd_ok, 1)

            for h in range(2 * NH):
                nc.gpsimd.memset(nslope[:, h:h + 1], -slope(h))
            for i in range(8):
                nc.gpsimd.memset(firstw[:, i:i + 1], float(8 - i))
            link(nc.gpsimd.iota(rel_dsa[:, :], pattern=[[-1, SEQ]], base=P, channel_multiplier=1,
                                allow_small_or_imprecise_dtypes=True))
            link(nc.gpsimd.affine_select(out=rel_swa[:, :], in_=rel_dsa[:, :], compare_op=ALU.is_ge, fill=FAR,
                                         base=-1, pattern=[[1, SEQ]], channel_multiplier=-1))
            link(nc.gpsimd.affine_select(out=rel_swa[:, :], in_=rel_swa[:, :], compare_op=ALU.is_ge, fill=FAR,
                                         base=P, pattern=[[-1, SEQ]], channel_multiplier=1))
            link(nc.gpsimd.affine_select(out=rel_dsa[:, :], in_=rel_dsa[:, :], compare_op=ALU.is_ge, fill=FAR,
                                         base=P, pattern=[[-1, SEQ]], channel_multiplier=1))
            link(nc.gpsimd.memset(causal[:, :], 3.0e38))
            link(nc.gpsimd.affine_select(out=causal[:, :], in_=causal[:, :], compare_op=ALU.is_ge, fill=NONCAUSAL,
                                         base=P, pattern=[[-1, SEQ]], channel_multiplier=1))
            link(nc.gpsimd.memset(tri[:, :], 1.0))
            link(nc.gpsimd.affine_select(out=tri[:, :], in_=tri[:, :], compare_op=ALU.is_ge, fill=0.0, base=0,
                                         pattern=[[1, P]], channel_multiplier=-1))
            nc.gpsimd.memset(score[:, :, :], 0.0)
            nc.gpsimd.iota(iota[:, :], pattern=[[1, P]], base=0, channel_multiplier=0,
                           allow_small_or_imprecise_dtypes=True).then_inc(consts, 1)

            for j in range(4):
                for h in range(2):
                    ada_piece(2, 0, j, h, CREDIT + 2 * j + h - 1 if j else None)
            ada_section(0, c0=1)
            ada_section(1)
            pool.wait_ge(qk_ms, 1)
            power(qk_rstd[:, :, :].rearrange("p t h -> p (t h)"), NT * N_RMS, qk_pow)
            ada_section(2)
            ada_section(3)
            pool.wait_ge(ms_ok, 2)
            nc.gpsimd.tensor_tensor(stat[:, 4:6], stat[:, 2:4], mhalf[:, 0:1].broadcast_to([P, NT]), ALU.pow
                                    ).then_inc(rstd_ok, 1)

        @block.tensor
        def _(pe):
            for credited in (qT_bank, e_tr, split_used):
                pe.sem_inc(credited, CREDIT)

            def reduce_to_columns(acc, b, o):
                for k in range(KC):
                    mm = nc.tensor.matmul(bank[b][:, o + k:o + k + 1], chunk_cols(acc, k // 4, k % 4), ones[:, 0:1],
                                          start=True, stop=True)
                mm.then_inc(ada_red, 1)

            def reduce_to_rows(acc, bias):
                for q in range(4):
                    nc.tensor.matmul(bank[4 + q][:, :], ones[:, :], acc[:, q * 512:(q + 1) * 512],
                                     start=True, stop=False)
                    mm = nc.tensor.matmul(bank[4 + q][:, :], ones[0:1, :], bias[:, q * 512:(q + 1) * 512],
                                          start=False, stop=True)
                mm.then_inc(ada_red, 1)

            def products(out, s, terms, cols_, start, stop):
                hi, lo = terms
                nc.tensor.matmul(out, hi, w_hi[:, s, cols_], start=start, stop=False)
                nc.tensor.matmul(out, lo, w_hi[:, s, cols_], start=False, stop=False)
                return nc.tensor.matmul(out, hi, w_lo[:, s, cols_], start=False, stop=stop)

            def chunk(base, unit, k, width, banks=range(4), lhs0=0, nk=KC):
                if banks[0] == 0:
                    pe.wait_ge(split_ok, base + (k + 1))
                half = width // 2
                for b in banks:
                    t, cb = b // 2, b % 2
                    if k == 0 and not (isinstance(unit, int) and unit == 0):
                        pe.wait_ge(unit_out, unit * 4 + (b - 3))
                    tokens = slice(t * P, (t + 1) * P)
                    mm = products(bank[b][:, 0:half], k % NSPLIT,
                                  (hT_hi[:, lhs0 + k, tokens], hT_lo[:, lhs0 + k, tokens]),
                                  slice(cb * half, (cb + 1) * half), k == 0, k == nk - 1)
                    if b == 3:
                        mm.then_inc(split_used, 1)
                    elif k == nk - 1:
                        mm.then_inc(unit_bank, 1)

            def heads_transposed(step, t):
                this = pe.compute_val(step + 1)
                pe.wait_ge(consts, 2)
                pe.wait_ge(staged, this)
                for r in range(GQ):
                    mm = nc.tensor.transpose(bank[6][0:HD, r * P:(r + 1) * P], stage[:, t, r * HD:(r + 1) * HD],
                                             ident[:, :])
                mm.then_inc(qT_bank, 1)

            def scores(step, t, keys):
                pe.wait_ge(qT_out, step + 1)
                nk = P * (t + 1)
                for r in range(GQ):
                    b, o = (4 + r // 2, (r % 2) * SEQ) if t else (4, r * P)
                    mm = nc.tensor.matmul(bank[b][:, o:o + nk], qT[:, r * P:(r + 1) * P], keys[:, 0:nk],
                                          start=True, stop=True)
                mm.then_inc(s_bank, 1)

            pe.wait_ge(consts, 2)
            for n in range(8):
                t, c_ = n // 4, n % 4
                if n % 4 == 0:
                    pe.wait_ge(xhat_ok, t + 1)
                for j in range(4):
                    mm = nc.tensor.transpose(bank[n][:, j * P:(j + 1) * P], chunk_cols(x_raw[:, t, :], c_, j),
                                             ident[:, :])
                mm.then_inc(xT_bank, 1)
            pe.wait_ge(xT_out, 8)
            pe.wait_ge(ada0_used, CREDIT + KC)
            reduce_to_columns(ada_a, 0, 0)
            pe.wait_ge(ada0_used, CREDIT + 2 * KC)
            reduce_to_columns(ada_b, 0, KC)

            for u in range(2):
                for k in range(KC):
                    if u == 0:
                        pe.wait_ge(h_ready, k + 1)
                    chunk(KC * u, u, k, UW)
            pe.wait_ge(ada_used, CREDIT + ADA_SECTION)
            pe.wait_ge(in_brow, 16)
            reduce_to_rows(ada_a, brow1)
            pe.wait_ge(ada_done, 1)
            pe.wait_ge(unit_out, 4)
            for t in range(NT):
                mm = nc.tensor.transpose(bank[6][0:HD, t * P:(t + 1) * P], proj[:, t, KI:KI + HD], ident[:, :])
            mm.then_inc(kT_bank, 1)
            pe.wait_ge(kT_out, 1)

            with pe.Fori(0, 2) as v:
                base = v * KC + 2 * KC
                for s in range(4):
                    t, step, k = s % 2, v * 4 + s, 4 * s
                    chunk(base, v + 2, k, UW, (0, 1))
                    heads_transposed(step, t)
                    chunk(base, v + 2, k, UW, (2, 3))
                    pe.wait_ge(kT_out, 1)
                    pe.wait_ge(relu_out, CREDIT + step)
                    scores(step, t, kT[:, 0, :])
                    for kk in range(k + 1, k + 4):
                        chunk(base, v + 2, kk, UW)

            pe.wait_ge(k_norm, 1)
            pe.wait_ge(relu_out, CREDIT + IDX_STEPS)
            for hk in range(1 + KVH):
                for t in range(NT):
                    o = (hk % 2) * SEQ + t * P
                    mm = nc.tensor.transpose(bank[4 + hk // 2][0:HD, o:o + P], kn[:, t, hk * HD:(hk + 1) * HD],
                                             ident[:, :])
            mm.then_inc(kT_bank, 1)
            pe.wait_ge(ada_used, CREDIT + 2 * ADA_SECTION)
            reduce_to_columns(ada_b, 7, 0)
            pe.wait_ge(ada_done, 2)
            pe.wait_ge(kT_out, 2)

            with pe.Fori(0, N_UNITS_GATE) as u:
                base, unit = u * KC + K_GATE, u + N_UNITS_PROJ
                for s in range(4):
                    t, swa, k = s % 2, s < 2, 4 * s
                    a = u * 4 + s
                    step = u * 4 + (s + IDX_STEPS)
                    chunk(base, unit, k, GW, (0, 1))
                    heads_transposed(step, t)
                    chunk(base, unit, k, GW, (2, 3))
                    pe.wait_ge(kT_out, 2)
                    pe.wait_ge(pT_out, CREDIT + a)
                    keys = kT[:, bass.ds(u + 2, 1), :].rearrange("d a s -> d (a s)") if swa else kT[:, 1, :]
                    scores(step, t, keys)
                    chunk(base, unit, k + 1, GW)
                    chunk(base, unit, k + 2, GW)
                    chunk(base, unit, k + 3, GW, (0, 1))
                    pe.wait_ge(exp_ok, a + 1)
                    for kt in range(t + 1):
                        for r in range(GQ):
                            mm = nc.tensor.transpose(bank[4 + kt][:, r * P:(r + 1) * P],
                                                     prob[:, r * SEQ + kt * P:r * SEQ + (kt + 1) * P], ident[:, :])
                    mm.then_inc(pT_bank, 1)
                    chunk(base, unit, k + 3, GW, (2, 3))
                    pe.wait_ge(pT_out, CREDIT + a + 1)
                    pe.wait_ge(o_out, CREDIT + a)
                    v_cols = bass.ds(u * HD + VA, HD) if swa else slice(VB, VB + HD)
                    for r in range(GQ):
                        for kt in range(t + 1):
                            o = kt * GQ * P + r * P
                            mm = nc.tensor.matmul(bank[7][:, r * HD:(r + 1) * HD], probT[:, o:o + P],
                                                  proj[:, kt, v_cols], start=(kt == 0), stop=(kt == t))
                    mm.then_inc(o_bank, 1)

            pe.wait_ge(o_out, CREDIT + ATT_STEPS)
            pe.wait_ge(ada_used, CREDIT + 3 * ADA_SECTION)
            reduce_to_columns(ada_b, 7, 0)

            def transposes(first, source):
                for n in range(8):
                    if first + n >= 3:
                        pe.wait_ge(t_out, first + n - 2)
                    for m in range(4):
                        mm = nc.tensor.transpose(bank[4 + (first + n) % 3][:, m * P:(m + 1) * P], source(n, m),
                                                 ident[:, :])
                    mm.then_inc(t_bank, 1)

            def outputs_of(n, m):
                pair = 4 * (n // 2) + m
                o = QA + pair * P if pair < 8 else QB + (pair - 8) * P
                return proj[:, n % 2, o:o + P]

            transposes(0, outputs_of)
            pe.wait_ge(t_out, 8)
            for nu in range(4):
                for k in range(8):
                    chunk(K_BRANCH + 8 * nu, BRANCH0 + nu, k, GW, lhs0=8 * (nu // 2), nk=8)

            def merged_of(n, m):
                if m == 0:
                    pe.wait_ge(merged, 4 if n < 4 else 8)
                return chunk_cols(gates[:, n % 2, 0:D], n // 2, m)

            transposes(8, merged_of)
            pe.wait_ge(t_out, 16)
            for u in range(2):
                for k in range(KC):
                    chunk(K_OUT + KC * u, OUT0 + u, k, GW)
            pe.wait_ge(ada_used, CREDIT + 4 * ADA_SECTION)
            pe.wait_ge(in_brow, 32)
            pe.wait_ge(ada_done, 3)
            reduce_to_rows(ada_b, brow2)

            pe.wait_ge(diag_ok, 1)
            for n in range(8):
                if n >= 4:
                    pe.wait_ge(h2_out, n - 3)
                for j in range(4):
                    mm = nc.tensor.matmul(bank[n % 4][:, j * P:(j + 1) * P], chunk_cols(x1[:, n % 2, :], n // 2, j),
                                          hot_s[:, n % 2, :], start=True, stop=True)
                mm.then_inc(h2_bank, 1)
            pe.wait_ge(h2_out, 8)
            pe.wait_ge(ada_done, 4)
            pe.wait_ge(in_small, SMALL)
            for t in range(NT):
                for k in range(KC):
                    mm = nc.tensor.matmul(bank[4][:, t * 64:t * 64 + NG + NE], h2T[:, k, t * P:(t + 1) * P],
                                          w_route[:, k, :], start=(k == 0), stop=(k == KC - 1))
            mm.then_inc(logit_bank, 1)
            pe.wait_ge(onehot_ok, 1)
            pe.wait_ge(consts, 3)
            nc.tensor.matmul(bank[5][:, 0:NG], tri[:, :], onehot[:, 0, :], start=True, stop=True)
            nc.tensor.matmul(bank[5][:, NG:2 * NG], tri[:, :], onehot[:, 1, :], start=True, stop=False)
            nc.tensor.matmul(bank[5][:, NG:2 * NG], ones[:, :], onehot[:, 0, :], start=False, stop=True)
            nc.tensor.matmul(bank[5][:, 2 * NG:3 * NG], ones[:, :], onehot[:, 0, :], start=True, stop=False)
            nc.tensor.matmul(bank[5][:, 2 * NG:3 * NG], ones[:, :], onehot[:, 1, :], start=False, stop=True
                             ).then_inc(rank_bank, 1)

            def gather_rows(n):
                pe.wait_ge(g_hot, n + 1)
                for q in range(4):
                    if q >= 2:
                        pe.wait_ge(g_out, n * 4 + (q - 1))
                    for j in range(4):
                        for t in range(NT):
                            mm = nc.tensor.matmul(bank[7 - q % 2][:, j * P:(j + 1) * P], chunk_cols(x1[:, t, :], q, j),
                                                  hot_s[:, t, :], start=(t == 0), stop=(t == NT - 1))
                    mm.then_inc(g_bank, 1)

            def gather_routing(n, g):
                pe.wait_ge(g_out, n * 4 + 4)
                for t in range(NT):
                    nc.tensor.transpose(bank[6][:, t * P:(t + 1) * P], hot[:, t, :], ident[:, :])
                for t in range(NT):
                    mm = nc.tensor.matmul(bank[6][:, SEQ:SEQ + EPG], hot[:, t, :],
                                          comb[:, t, bass.ds(g * EPG, EPG)], start=(t == 0), stop=(t == NT - 1))
                mm.then_inc(g_hotT, 1)

            def act_transposed(ne):
                pe.wait_ge(consts, 2)
                pe.wait_ge(e_act, CREDIT + ne + 1)
                for m in range(4):
                    mm = nc.tensor.transpose(bank[7][:, m * P:(m + 1) * P], act_o[:, m * P:(m + 1) * P], ident[:, :])
                mm.then_inc(e_tr, 1)

            def gate_up(ne, before=True):
                pe.wait_ge(e_act, CREDIT + ne)
                for h in range(16):
                    if h == 8 and before:
                        act_transposed(ne - 1)
                    b, d0 = 4 + h // 8, 2 * (h % 8)
                    pe.wait_ge(split_ok, ne * 16 + (K_MOE + h + 1))
                    for j in range(2):
                        d = d0 + j
                        mm = products(bank[b][:, :], h % NSPLIT, (hG_hi[:, d, :], hG_lo[:, d, :]),
                                      slice(j * FE, (j + 1) * FE), d == 0, d == KC - 1)
                    mm.then_inc(split_used, 1)

            def down(ne, first=False, last=False):
                pe.wait_ge(e_trout, ne + 1)
                for m in range(4):
                    pe.wait_ge(down_landed[m], ne * 16 + 16)
                    for q in range(4):
                        mm = nc.tensor.matmul(bank[q][:, :], actT[:, m * P:(m + 1) * P],
                                              down_slot[m][:, q * 512:(q + 1) * 512],
                                              start=(first and m == 0), stop=(last and m == 3))
                        if last and m == 3 and q < 3:
                            mm.then_inc(y_bank, 1)
                    mm.then_inc(d_used, 1)

            def scatter(n):
                pe.wait_ge(y_out, n * 4 + 4)
                for t in range(NT):
                    for q in range(4):
                        if t:
                            pe.wait_ge(sc_out, CREDIT + n * 8 + (q + 1))
                        nc.tensor.matmul(bank[q][:, :], hotT[:, t * P:(t + 1) * P], y_sb[:, q * 512:(q + 1) * 512],
                                         start=True, stop=True).then_inc(sc_bank, 1)

            def group(n, ne, following):
                pe.wait_ge(g_hotT_out, n + 1)
                gate_up(ne, before=False)
                gate_up(ne + 1)
                pe.wait_ge(sc_out, CREDIT + n * 8)
                down(ne, first=True)
                with pe.Fori(2, EPG) as e:
                    gate_up(ne + e)
                    down(ne + e - 1)
                if following:
                    gather_rows(n + 1)
                    pe.wait_ge(g_out, n * 4 + 7)
                act_transposed(ne + 7)
                down(ne + 7, last=True)
                scatter(n)

            def moe_pass(ps):
                n0 = ps * NG
                gather_rows(n0)
                gather_routing(n0, 0)
                with pe.Fori(0, NG - 1) as g:
                    group(g + n0, g * EPG + n0 * EPG, True)
                    gather_routing(g + (n0 + 1), g + 1)
                group(n0 + NG - 1, (n0 + NG - 1) * EPG, False)

            moe_pass(0)
            pe.wait_ge(route_ok, 1)
            over = pe.value_load(flag[0:1, 0:1], min_val=0, max_val=1)
            with pe.If(over > 0):
                moe_pass(1)

        @block.scalar
        def _(act):
            for credited in (relu_out, pT_out):
                act.sem_inc(credited, CREDIT)

            def round_half(src, s, free):
                if free is not None:
                    act.wait_ge(split_used, free)
                nc.scalar.activation(w_hi[:, s, :], src, ACT.Copy).then_inc(hi_ok, 1)

            def round_dense(base, i):
                if i % 2 == 0:
                    act.wait_ge(landed[(i // 2) % RING], base * 2 + 16 * (ROUND0 + 1 + i // 8))
                round_half(dense_half(i), i % NSPLIT,
                           None if isinstance(base, int) and base + i < NSPLIT - 1
                           else base + (CREDIT + i + 1 - NSPLIT))

            def round_moe(ne, h, fresh=False):
                if h >= 16:
                    ne, h = ne + 1, h - 16
                if h % 2 == 0:
                    if h < 8:
                        act.wait_ge(gate_landed[h // 2], ne * 16 + 16)
                    else:
                        act.wait_ge(landed[(h - 8) // 2], ne * 16 + 16 * (ROUND0 + K_MOE // 8 + 1))
                round_half(moe_half(h), h % NSPLIT, ne * 16 + (K_MOE + CREDIT + h + 1 - NSPLIT))

            def take_unit(unit, store):
                for b in range(4):
                    if b < 3:
                        act.wait_ge(unit_bank, unit * 3 + (b + 1))
                    else:
                        act.wait_ge(split_used, unit * KC + (CREDIT + KC))
                    store(b, b // 2, b % 2).then_inc(unit_out, 1)

            act.dma_start(cond[:, :].rearrange("p (c j) -> p c j", j=4), c[0].rearrange("(c p j) -> p c j", p=P, j=4)
                          ).then_inc(in_c, 16)
            for t in range(NT):
                act.dma_start(x_raw[:, t, :], x_v[:, t, :]).then_inc(in_x, 16)

            def load(dst, src):
                act.dma_start(dst, src).then_inc(in_small, 16)

            def chunk_col(i):
                return cols[:, i, :].rearrange("p (c j) -> p c j", j=4)

            load(chunk_col(C_LN1), ln1_g[0].rearrange("(c p j) -> p c j", p=P, j=4))
            load(chunk_col(C_LN2), ln2_g[0].rearrange("(c p j) -> p c j", p=P, j=4))
            for i, s in ((C_BSH1, 0), (C_BSC1, 1), (C_BSH2, 3), (C_BSC2, 4)):
                load(chunk_col(i), bias_v[:, s, :, :])
            for i, g in enumerate((swa_q_norm, swa_k_norm, dsa_q_norm, dsa_k_norm)):
                load(gain_in[:, i:i + 1], g[0].rearrange("(d a) -> d a", a=1))
            load(sinks[:, :], swa_sinks[0:1, :].broadcast_to([P, NH]))
            load(b_route[:, 0:NG], b_group[0:1, :].broadcast_to([P, NG]))
            load(b_route[:, NG:], b_expert[0:1, :].broadcast_to([P, NE]))
            wr = w_route[:, :, :].rearrange("p (c j) n -> p c j n", j=4)
            for c_ in range(4):
                load(wr[:, c_, :, 0:NG], w_group[0].rearrange("(c p j) n -> p c j n", p=P, j=4)[:, c_, :, :])
            for c_ in range(4):
                load(wr[:, c_, :, NG:], w_expert[0].rearrange("(c p j) n -> p c j n", p=P, j=4)[:, c_, :, :])

            act.wait_ge(in_c, 16)
            nc.scalar.activation(condr[:, :], cond[:, :], ACT.Exp, scale=-1.0).then_inc(silu_e, 1)
            act.wait_ge(in_x, 32)
            for t in range(NT):
                nc.scalar.activation(proj[:, t, 0:D], x_raw[:, t, :], ACT.Square, accum_out=stat[:, t:t + 1]
                                     ).then_inc(sq_done, 1)
            for n in range(8):
                t, c_ = n // 4, n % 4
                act.wait_ge(xT_bank, n + 1)
                nc.scalar.activation(xT_raw[:, t, 4 * c_:4 * c_ + 4, :],
                                     bank[n][:, :].rearrange("p (j s) -> p j s", j=4), ACT.Copy).then_inc(xT_out, 1)

            def round_h(k):
                act.wait_ge(h_raw, k + 1)
                nc.scalar.activation(hT_hi[:, k, :].rearrange("p (t s) -> p t s", t=NT), xT_raw[:, :, k, :], ACT.Copy
                                     ).then_inc(h_hi, 1)

            for k in range(4):
                round_h(k)
            for i in range(LEAD):
                round_dense(0, i)
            for k in range(4, KC):
                round_h(k)

            def to_proj(c0):
                half = UW // 2
                return lambda b, t, cb: nc.scalar.activation(proj[:, t, bass.ds(c0 + cb * half, half)],
                                                             bank[b][:, 0:half], ACT.Copy)

            with act.Fori(0, 2) as u:
                for i in range(KC):
                    round_dense(u * KC, LEAD + i)
                take_unit(u, to_proj(u * (-UW) + (PROJ - UW)))
            act.wait_ge(h_ready, KC)
            act.dma_start(brow1, b_ada[0:1, 2 * D:3 * D]).then_inc(in_brow, 16)

            def take_queries(step):
                act.wait_ge(qT_bank, CREDIT + step + 1)
                nc.scalar.activation(qT[:, :], bank[6][0:HD, :], ACT.Copy).then_inc(qT_out, 1)

            act.wait_ge(unit_out, 8)
            with act.Fori(0, 2) as v:
                for s in range(4):
                    t, step = s % 2, v * 4 + s
                    nc.scalar.activation(stage[:, t, :], proj[:, t, bass.ds(v * (2 * GQ * HD) + (QI + (s // 2) * GQ * HD),
                                                                            GQ * HD)], ACT.Copy).then_inc(staged, 1)
                    round_dense(v * KC + 2 * KC, 4 * s + LEAD)
                    take_queries(step)
                    round_dense(v * KC + 2 * KC, 4 * s + LEAD + 1)
                    act.wait_ge(s_bank, step + 1)
                    act.wait_ge(relu_used, CREDIT + step)
                    if t:
                        nc.scalar.activation(relu_s[:, t, 0:512], bank[4][:, :], ACT.Relu, scale=HD ** -0.5)
                        nc.scalar.activation(relu_s[:, t, 512:1024], bank[5][:, :], ACT.Relu, scale=HD ** -0.5
                                             ).then_inc(relu_out, 1)
                    else:
                        nc.scalar.activation(relu_s[:, t, 0:512], bank[4][:, :], ACT.Relu, scale=HD ** -0.5
                                             ).then_inc(relu_out, 1)
                    round_dense(v * KC + 2 * KC, 4 * s + LEAD + 2)
                    round_dense(v * KC + 2 * KC, 4 * s + LEAD + 3)
                take_unit(v + 2, to_proj(v * (-UW) + (PROJ - 3 * UW)))

            with act.Fori(0, N_UNITS_GATE) as u:
                base = u * KC + K_GATE
                for s in range(4):
                    t, swa, a = s % 2, s < 2, u * 4 + s
                    round_dense(base, 4 * s + LEAD)
                    take_queries(u * 4 + (s + IDX_STEPS))
                    round_dense(base, 4 * s + LEAD + 1)
                    act.wait_ge(max_ok, a + 1)
                    nk = P * (t + 1)
                    for r in range(GQ):
                        p = prob[:, r * SEQ:r * SEQ + nk]
                        ins = nc.scalar.activation(p, p, ACT.Exp, bias=sm[:, 1, r:r + 1], accum_out=sm[:, 2, r:r + 1])
                    if swa:
                        ins = nc.scalar.activation(sm[:, 4, :], sm[:, 3, :], ACT.Exp)
                    ins.then_inc(exp_ok, 1)
                    round_dense(base, 4 * s + LEAD + 2)
                    act.wait_ge(pT_bank, a + 1)
                    for kt in range(t + 1):
                        ins = nc.scalar.activation(probT[:, kt * GQ * P:(kt + 1) * GQ * P], bank[4 + kt][:, :], ACT.Copy)
                    ins.then_inc(pT_out, 1)
                    round_dense(base, 4 * s + LEAD + 3)
                take_unit(u + N_UNITS_PROJ,
                          lambda b, t, cb: nc.scalar.activation(gates[:, t, bass.ds(u * GW + cb * 512, 512)],
                                                                bank[b][:, :], ACT.Exp, scale=-1.0))

            def take_transposes(first):
                for n in range(8):
                    act.wait_ge(t_bank, first + n + 1)
                    k = 4 * (n // 2)
                    nc.scalar.activation(hT_hi[:, k:k + 4, (n % 2) * P:(n % 2 + 1) * P],
                                         bank[4 + (first + n) % 3][:, :].rearrange("p (j s) -> p j s", j=4), ACT.Copy
                                         ).then_inc(t_hi, 1)

            take_transposes(0)
            for t in range(NT):
                act.dma_start(x1[:, t, :], x_v[:, t, :]).then_inc(in_x1, 16)
            act.dma_start(brow2, b_ada[0:1, 5 * D:6 * D]).then_inc(in_brow, 16)
            act.wait_ge(unit_out, 4 * UNITS)
            for nu in range(4):
                for i in range(8):
                    if i % 2 == 0:
                        t, c0 = i // 4, (nu // 2) * D + (nu % 2) * GW + (i // 2 % 2) * 512
                        g = gates[:, t, c0:c0 + 512]
                        nc.scalar.activation(g, g, ACT.Copy, bias=1.0).then_inc(gate_sum, 1)
                    round_dense(K_BRANCH + 8 * nu, LEAD + i)
            take_transposes(8)
            for i in range(2 * KC):
                if LEAD + i < 2 * KC:
                    round_dense(K_OUT, LEAD + i)
                else:
                    round_moe(0, LEAD + i - 2 * KC)
            act.wait_ge(x1_ok, 8)
            for t in range(NT):
                sq = h2T[:, t * 8:(t + 1) * 8, :].rearrange("p k s -> p (k s)")
                nc.scalar.activation(sq, x1[:, t, :], ACT.Square, accum_out=stat[:, t:t + 1]).then_inc(sq_done, 1)
            act.wait_ge(r_sub, 1)
            nc.scalar.activation(rt[:, 4, :, 0:NG], rt[:, 3, :, 0:NG], ACT.Exp).then_inc(r_exp, 1)
            act.wait_ge(r_sub, 2)
            nc.scalar.activation(rt[:, 11, :, 0:1], rt[:, 10, :, 0:1], ACT.Exp).then_inc(r_exp, 1)

            def gate_exp(ne):
                act.wait_ge(split_used, ne * 16 + (CREDIT + K_MOE + 8))
                act.wait_ge(e_act, CREDIT + ne)
                nc.scalar.activation(act_e, bank[4][:, :], ACT.Exp, scale=-1.0).then_inc(e_exp, 1)
                act.wait_ge(e_exp, ne * 2 + 1)
                nc.scalar.activation(act_e, act_e, ACT.Copy, bias=1.0).then_inc(e_exp, 1)

            def take_act(ne):
                act.wait_ge(e_tr, CREDIT + ne + 1)
                nc.scalar.activation(actT, bank[7][:, :], ACT.Copy).then_inc(e_trout, 1)

            def expert(ne, before=True, following=True):
                for h in range(LEAD, 16 + LEAD if following else 16):
                    round_moe(ne, h)
                    if h == 8 + LEAD:
                        gate_exp(ne)
                        if before:
                            take_act(ne - 1)

            def group(n, ne, following):
                expert(ne, before=False)
                with act.Fori(1, EPG - 1) as e:
                    expert(ne + e)
                expert(ne + (EPG - 1), following=following)
                take_act(ne + (EPG - 1))
                for q in range(4):
                    if q < 3:
                        act.wait_ge(y_bank, n * 3 + (q + 1))
                    else:
                        act.wait_ge(d_used, ne * 4 + 4 * EPG)
                    nc.scalar.activation(y_sb[:, q * 512:(q + 1) * 512], bank[q][:, :], ACT.Copy).then_inc(y_out, 1)

            def moe_pass(ps):
                n0 = ps * NG
                with act.Fori(0, NG - 1) as g:
                    group(g + n0, g * EPG + n0 * EPG, True)
                group(n0 + NG - 1, (n0 + NG - 1) * EPG, False)

            moe_pass(0)
            act.wait_ge(route_ok, 1)
            over = act.value_load(flag[0:1, 0:1], min_val=0, max_val=1)
            with act.If(over > 0):
                for h in range(LEAD):
                    round_moe(NE, h)
                moe_pass(1)

        @block.vector
        def _(ve):
            for credited in (ada0_used, ada_used, relu_used, o_out, e_act, sc_out):
                ve.sem_inc(credited, CREDIT)
            own = Own(ve, dve_own)
            add, wait = own.add, own.wait
            v_ = nc.vector

            def remainder(src, s, number):
                ve.wait_ge(hi_ok, number + 1)
                v_.tensor_tensor(w_lo[:, s, :], src, w_hi[:, s, :].bitcast(F32), ALU.subtract).then_inc(split_ok, 1)

            def remainder_dense(base, i):
                remainder(dense_half(i), i % NSPLIT, base + i)

            def remainder_moe(ne, h):
                remainder(moe_half(h % 16), h % NSPLIT, ne * 16 + (K_MOE + h))

            def column(k):
                return bass.ds(k, 1)

            def sum_piece(acc, src, k, used, n):
                ve.wait_ge(used, CREDIT + n)
                v_.scalar_tensor_tensor(out=acc, in0=src, scalar=cond[:, k], in1=acc,
                                        op0=ALU.mult, op1=ALU.add).then_inc(used, 1)

            def sum_half(acc, base, i):
                section, k0 = base
                h = i % 2
                ve.wait_ge(ada_landed[h], k0 * 16 + 16 * (section * KC + i // 2 + 1))
                sum_piece(acc[:, h * HALF:(h + 1) * HALF], ada_ring[:, h, :], column(k0 + i // 2), ada_used,
                          k0 * 2 + (section * ADA_SECTION + i))

            ve.wait_ge(silu_e, 1)
            add(v_.tensor_scalar(condr[:, :], condr[:, :], 1.0, None, ALU.add))
            wait()
            add(v_.reciprocal(condr[:, :], condr[:, :]))
            wait()
            add(v_.tensor_tensor(cond[:, :], cond[:, :], condr[:, :], ALU.mult))

            def mean_squares(done):
                ve.wait_ge(sq_done, done)
                v_.tensor_scalar(stat[:, 2:4], stat[:, 0:2], 1.0 / D, EPS, ALU.mult, ALU.add).then_inc(ms_ok, 1)
                ve.wait_ge(rstd_ok, done // 2)

            mean_squares(2)
            for t in range(NT):
                v_.tensor_scalar(x_raw[:, t, :], x_raw[:, t, :], stat[:, 4 + t:5 + t], None, ALU.mult
                                 ).then_inc(xhat_ok, 1)
            wait()
            ve.wait_ge(consts, 2)
            for s, acc in enumerate((ada_a, ada_b)):
                for k in range(KC):
                    ve.wait_ge(landed[k % RING], 16 * (s * (KC // RING) + k // RING + 1))
                    sum_piece(acc[:, :], ring[:, k % RING, :], column(k), ada0_used, s * KC + k)
            ve.wait_ge(in_small, SMALL)
            ve.wait_ge(ada_red, 2)
            add(v_.tensor_tensor(cols[:, C_S1, :], bank[0][:, 0:KC], cols[:, C_BSH1, :], ALU.add))
            add(v_.tensor_tensor(cols[:, C_A1, :], bank[0][:, KC:2 * KC], cols[:, C_BSC1, :], ALU.add))
            wait()
            add(v_.scalar_tensor_tensor(out=cols[:, C_A1, :], in0=cols[:, C_A1, :], scalar=1.0, in1=cols[:, C_LN1, :],
                                        op0=ALU.add, op1=ALU.mult))
            wait()
            ve.wait_ge(xT_out, 8)

            def h_chunks(ks):
                for k in ks:
                    v_.tensor_scalar(xT_raw[:, :, k, :], xT_raw[:, :, k, :], cols[:, C_A1, k:k + 1],
                                     cols[:, C_S1, k:k + 1], ALU.mult, ALU.add).then_inc(h_raw, 1)
                for k in ks:
                    ve.wait_ge(h_hi, k + 1)
                    v_.tensor_tensor(hT_lo[:, k, :].rearrange("p (t s) -> p t s", t=NT), xT_raw[:, :, k, :],
                                     hT_hi[:, k, :].bitcast(F32).rearrange("p (t s) -> p t s", t=NT), ALU.subtract
                                     ).then_inc(h_ready, 1)

            h_chunks(range(4))
            for i in range(LEAD):
                remainder_dense(0, i)
            h_chunks(range(4, KC))
            for m in range(2):
                add(v_.tensor_tensor(gain_k[:, m:m + 1], gain_in[:, 2 * m:2 * m + 1], gain_in[:, 2 * m + 1:2 * m + 2],
                                     ALU.mult))
            wait()
            add(v_.tensor_scalar(gain_k[:, :], gain_k[:, :], HD ** -0.5, None, ALU.mult))
            add(v_.memset(ada_a[:, :], 0.0))
            wait()
            with ve.Fori(0, 2) as u:
                for i in range(KC):
                    remainder_dense(u * KC, LEAD + i)
                    sum_half(ada_a, (0, u * 8), i)

            def take_rows(acc, red):
                ve.wait_ge(ada_red, red)
                for q in range(4):
                    ins = v_.tensor_copy(acc[:, q * 512:(q + 1) * 512], bank[4 + q][:, :])
                ins.then_inc(ada_done, 1)

            take_rows(ada_a, 3)
            ve.wait_ge(unit_out, 4)
            add(v_.tensor_scalar(wi4[:, :, :], proj[:, :, WI:WI + NH], NH ** -0.5, None, ALU.mult))
            ve.wait_ge(kT_bank, 1)
            v_.tensor_copy(kT[:, 0, :], bank[6][0:HD, 0:SEQ]).then_inc(kT_out, 1)
            add(v_.memset(ada_b[:, :], 0.0))
            ve.wait_ge(consts, 3)
            wait()
            IDX_ADDS = 4 * (GQ - 1)
            with ve.Fori(0, 2) as v:
                own.enter(v, IDX_ADDS)
                for s in range(4):
                    t, nk = s % 2, P * (s % 2 + 1)
                    for i in range(4 * s, 4 * s + 4):
                        remainder_dense(v * KC + 2 * KC, LEAD + i)
                        sum_half(ada_b, (1, v * 8), i)
                        if i == 4 * s + 1:
                            ve.wait_ge(relu_out, CREDIT + v * 4 + (s + 1))
                            for r in range(GQ):
                                if r:
                                    wait()
                                else:
                                    ve.wait_ge(relu_used, CREDIT + v * 4 + s)
                                ins = v_.scalar_tensor_tensor(
                                    out=score[:, t, 0:nk], in0=relu_s[:, t, r * nk:(r + 1) * nk],
                                    scalar=wi4[:, t, bass.ds(v * 8 + (4 * (s // 2) + r), 1)],
                                    in1=score[:, t, 0:nk], op0=ALU.mult, op1=ALU.add)
                                if r < GQ - 1:
                                    add(ins)
                            ins.then_inc(relu_used, 1)
                own.leave(2, IDX_ADDS)
            ve.wait_ge(unit_out, 4 * N_UNITS_PROJ)
            ve.wait_ge(relu_used, CREDIT + IDX_STEPS)
            for lo, heads, at_ in ((QA, NH + KVH, 0), (QB, NH + 1, NH + KVH)):
                for t in range(NT):
                    src = proj[:, t, lo:lo + heads * HD]
                    add(v_.tensor_tensor(squares[:, 0:heads * HD], src, src, ALU.mult))
                    wait()
                    add(v_.tensor_reduce(qk_rstd[:, t, at_:at_ + heads],
                                         squares[:, 0:heads * HD].rearrange("p (h d) -> p h d", d=HD), AX, ALU.add))
                    wait()
            v_.tensor_scalar(qk_rstd[:, :, :], qk_rstd[:, :, :], 1.0 / HD, EPS, ALU.mult, ALU.add).then_inc(qk_ms, 1)

            for t in range(NT):
                nk = P * (t + 1)
                add(v_.tensor_tensor(score[:, t, 0:nk], score[:, t, 0:nk], causal[:, SEQ - nk:SEQ], ALU.min))
            wait()
            for t in range(NT):
                nk = P * (t + 1)
                for _ in range(TOPK // 8):
                    add(v_.max(top8[:, :], score[:, t, 0:nk]))
                    wait()
                    add(v_.match_replace(score[:, t, 0:nk], top8[:, :], score[:, t, 0:nk], TAKEN))
                    wait()
                add(v_.tensor_scalar(rel_top[:, t, 0:nk], score[:, t, 0:nk], 0.5 * (TAKEN + NONCAUSAL), FAR,
                                     ALU.is_ge, ALU.mult))
                wait()
                add(v_.tensor_tensor(rel_top[:, t, 0:nk], rel_top[:, t, 0:nk], rel_dsa[:, SEQ - nk:SEQ], ALU.max))

            ve.wait_ge(qk_pow, 1)
            for t in range(NT):
                add(v_.tensor_scalar(kn[:, t, 0:HD], proj[:, t, KB:KB + HD], qk_rstd[:, t, N_RMS - 1:N_RMS], None,
                                     ALU.mult))
                ins = v_.tensor_tensor(kn[:, t, HD:].rearrange("p (h d) -> p h d", d=HD),
                                       proj[:, t, KA:KA + KVH * HD].rearrange("p (h d) -> p h d", d=HD),
                                       qk_rstd[:, t, NH:NH + KVH].unsqueeze(2).broadcast_to([P, KVH, HD]), ALU.mult)
                if t == 0:
                    add(ins)
            ins.then_inc(k_norm, 1)
            ve.wait_ge(ada_red, 4)
            v_.tensor_tensor(cols[:, C_S2, :], bank[7][:, 0:KC], cols[:, C_BSH2, :], ALU.add).then_inc(ada_done, 1)
            ve.wait_ge(kT_bank, 2)
            for hk in range(1 + KVH):
                m = 1 if hk == 0 else 0
                ins = v_.tensor_scalar(kT[:, 1 + hk, :], bank[4 + hk // 2][0:HD, (hk % 2) * SEQ:(hk % 2 + 1) * SEQ],
                                       gain_k[:, m:m + 1], None, ALU.mult)
            ins.then_inc(kT_out, 1)
            add(v_.memset(ada_b[:, :], 0.0))
            wait()

            ATT_ADDS = 2 * (GQ + 5) + 2 * (GQ + 2)
            with ve.Fori(0, N_UNITS_GATE) as u:
                own.enter(u, ATT_ADDS)
                base = u * KC + K_GATE
                for s in range(4):
                    t, swa, a = s % 2, s < 2, u * 4 + s
                    nk = P * (t + 1)
                    q0, h0 = (QA, 0) if swa else (QB, NH + KVH)
                    heads = proj[:, t, bass.ds(u * (GQ * HD) + q0, GQ * HD)].rearrange("p (h d) -> p h d", d=HD)
                    ve.wait_ge(qT_bank, CREDIT + u * 4 + (s + IDX_STEPS))
                    v_.tensor_tensor(stage[:, t, :].rearrange("p (h d) -> p h d", d=HD), heads,
                                     qk_rstd[:, t, bass.ds(u * GQ + h0, GQ)].unsqueeze(2).broadcast_to([P, GQ, HD]),
                                     ALU.mult).then_inc(staged, 1)
                    remainder_dense(base, 4 * s + LEAD)
                    sum_half(ada_b, (2, u * 4), 2 * s)
                    ve.wait_ge(s_bank, u * 4 + (s + IDX_STEPS + 1))
                    for r in range(GQ):
                        b, o = (4 + r // 2, (r % 2) * SEQ) if t else (4, r * P)
                        rel = rel_swa[:, SEQ - nk:SEQ] if swa else rel_top[:, t, 0:nk]
                        add(v_.scalar_tensor_tensor(out=prob[:, r * SEQ:r * SEQ + nk], in0=rel,
                                                    scalar=nslope[:, bass.ds(u * GQ + ((0 if swa else NH) + r), 1)],
                                                    in1=bank[b][:, o:o + nk], op0=ALU.mult, op1=ALU.add))
                    wait()
                    p = prob.rearrange("p (r s) -> p r s", r=GQ)[:, :, 0:nk]
                    add(v_.tensor_reduce(sm[:, 0, :], p, AX, ALU.max))
                    wait()
                    if swa:
                        sink = sinks[:, bass.ds(u * GQ, GQ)]
                        add(v_.tensor_tensor(sm[:, 0, :], sm[:, 0, :], sink, ALU.max))
                        wait()
                        add(v_.tensor_tensor(sm[:, 3, :], sink, sm[:, 0, :], ALU.subtract))
                    v_.tensor_scalar(sm[:, 1, :], sm[:, 0, :], -1.0, None, ALU.mult).then_inc(max_ok, 1)
                    remainder_dense(base, 4 * s + LEAD + 1)
                    sum_half(ada_b, (2, u * 4), 2 * s + 1)
                    remainder_dense(base, 4 * s + LEAD + 2)
                    ve.wait_ge(exp_ok, a + 1)
                    if swa:
                        add(v_.tensor_tensor(sm[:, 5, :], sm[:, 2, :], sm[:, 4, :], ALU.add))
                        wait()
                    add(v_.reciprocal(sm[:, 6, :], sm[:, 5 if swa else 2, :]))
                    remainder_dense(base, 4 * s + LEAD + 3)
                    wait()
                    ve.wait_ge(o_bank, a + 1)
                    v_.tensor_tensor(heads, bank[7][:, 0:GQ * HD].rearrange("p (h d) -> p h d", d=HD),
                                     sm[:, 6, :].unsqueeze(2).broadcast_to([P, GQ, HD]), ALU.mult).then_inc(o_out, 1)
                own.leave(N_UNITS_GATE, ATT_ADDS)

            def take_transposes(first):
                for n in range(8):
                    ve.wait_ge(t_hi, first + n + 1)
                    k = 4 * (n // 2)
                    part_ = (slice(None), slice(k, k + 4), slice((n % 2) * P, (n % 2 + 1) * P))
                    v_.tensor_tensor(hT_lo[part_], bank[4 + (first + n) % 3][:, :].rearrange("p (j s) -> p j s", j=4),
                                     hT_hi[part_].bitcast(F32), ALU.subtract).then_inc(t_out, 1)

            ve.wait_ge(ada_red, 5)
            add(v_.tensor_tensor(cols[:, C_A2, :], bank[7][:, 0:KC], cols[:, C_BSC2, :], ALU.add))
            take_transposes(0)
            wait()
            v_.scalar_tensor_tensor(out=cols[:, C_A2, :], in0=cols[:, C_A2, :], scalar=1.0, in1=cols[:, C_LN2, :],
                                    op0=ALU.add, op1=ALU.mult).then_inc(ada_done, 1)
            add(v_.memset(ada_b[:, :], 0.0))
            wait()

            def unit_complete(b, unit, chunks):
                if b < 3:
                    ve.wait_ge(unit_bank, 3 * unit + b + 1)
                else:
                    ve.wait_ge(split_used, CREDIT + chunks)

            for nu in range(4):
                rnd, u = nu // 2, nu % 2
                for i in range(8):
                    remainder_dense(K_BRANCH + 8 * nu, LEAD + i)
                    b = i // 2
                    t, c0 = b // 2, u * GW + (b % 2) * 512
                    g = gates[:, t, rnd * D + c0:rnd * D + c0 + 512]
                    if i % 2 == 0:
                        sum_half(ada_b, (3, 0), 4 * nu + b)
                    else:
                        ve.wait_ge(gate_sum, 4 * nu + b + 1)
                        add(v_.reciprocal(g, g))
                wait()
                for b in range(4):
                    t, c0 = b // 2, u * GW + (b % 2) * 512
                    g = gates[:, t, rnd * D + c0:rnd * D + c0 + 512]
                    unit_complete(b, BRANCH0 + nu, K_BRANCH + 8 * (nu + 1))
                    v_.tensor_tensor(g, g, bank[b][:, :], ALU.mult).then_inc(unit_out, 1)
                if rnd:
                    for b in range(4):
                        t, c0 = b // 2, u * GW + (b % 2) * 512
                        g = gates[:, t, rnd * D + c0:rnd * D + c0 + 512]
                        ga = gates[:, t, c0:c0 + 512]
                        ve.wait_ge(unit_out, 4 * (BRANCH0 + nu) + b + 1)
                        v_.tensor_tensor(ga, ga, g, ALU.add).then_inc(merged, 1)
            take_transposes(8)
            ve.wait_ge(in_x1, 32)
            ve.wait_ge(ada_done, 1)
            for u in range(2):
                for i in range(KC):
                    if u * KC + LEAD + i < 2 * KC:
                        remainder_dense(K_OUT, u * KC + LEAD + i)
                    else:
                        remainder_moe(0, u * KC + LEAD + i - 2 * KC)
                    if i % 2 == 0:
                        sum_half(ada_b, (3, 0), 16 + 8 * u + i // 2)
                for b in range(4):
                    t, c0 = b // 2, u * GW + (b % 2) * 512
                    unit_complete(b, OUT0 + u, K_OUT + KC * (u + 1))
                    if u + b:
                        ve.wait_ge(x1_ok, 4 * u + b)
                    v_.tensor_tensor(tmp, bank[b][:, :], ada_a[:, c0:c0 + 512], ALU.mult).then_inc(unit_out, 1)
                    ve.wait_ge(unit_out, 4 * (OUT0 + u) + b + 1)
                    v_.tensor_tensor(x1[:, t, c0:c0 + 512], x1[:, t, c0:c0 + 512], tmp, ALU.add).then_inc(x1_ok, 1)
            mean_squares(4)
            for t in range(NT):
                ins = v_.tensor_scalar(hot_s[:, t, :], ident[:, :], stat[:, 4 + t:5 + t], None, ALU.mult)
            ins.then_inc(diag_ok, 1)
            take_rows(ada_b, 6)
            ve.wait_ge(ada_done, 4)

            def take_scaled(dst, b, c_, done):
                for j in range(4):
                    k = 4 * c_ + j
                    ins = v_.tensor_scalar(dst(k), bank[b][:, j * P:(j + 1) * P], cols[:, C_A2, k:k + 1],
                                           cols[:, C_S2, k:k + 1], ALU.mult, ALU.add)
                ins.then_inc(done, 1)

            for n in range(8):
                ve.wait_ge(h2_bank, n + 1)
                take_scaled(lambda k: h2T[:, k, (n % 2) * P:(n % 2 + 1) * P], n % 4, n // 2, h2_out)

            def r(i, w=8):
                return rt[:, i, :, 0:w]

            def wide(v, w):
                return v.broadcast_to([P, NT, w])

            def row(v, w):
                return v[:, 0:w].unsqueeze(1).broadcast_to([P, NT, w])

            def do(ins):
                add(ins)
                wait()

            def first_max(src, w, m, key, km, hot_out):
                do(v_.tensor_reduce(m, src, AX, ALU.max))
                do(v_.tensor_tensor(key, src, wide(m, w), ALU.is_equal))
                do(v_.tensor_tensor(key, key, row(firstw, w), ALU.mult))
                do(v_.tensor_reduce(km, key, AX, ALU.max))
                return v_.tensor_tensor(hot_out, key, wide(km, w), ALU.is_equal)

            ve.wait_ge(logit_bank, 1)
            do(v_.tensor_tensor(lg[:, :, :], bank[4][:, 0:2 * 64].rearrange("p (t n) -> p t n", t=NT)[:, :, 0:NG + NE],
                                row(b_route, NG + NE), ALU.add))
            gl = lg[:, :, 0:NG]
            first_max(gl, NG, r(0, 1), r(1, NG), r(2, 1), onehot[:, :, :]).then_inc(onehot_ok, 1)
            v_.tensor_tensor(r(3, NG), gl, wide(r(0, 1), NG), ALU.subtract).then_inc(r_sub, 1)
            ve.wait_ge(onehot_ok, 1)
            for t in range(NT):
                add(v_.tensor_tensor(esel[:, t, :].rearrange("p (g e) -> p g e", g=NG),
                                     lg[:, t, NG:].rearrange("p (g e) -> p g e", g=NG),
                                     onehot[:, t, :].unsqueeze(2).broadcast_to([P, NG, EPG]), ALU.mult))
            wait()
            for t in range(NT):
                add(v_.tensor_reduce(rt[:, 5, t, :], esel[:, t, :].rearrange("p (g e) -> p e g", g=NG), AX, ALU.add))
            wait()
            es = r(5)
            do(first_max(es, EPG, r(6, 1), r(7), r(2, 1), r(8)))
            do(v_.scalar_tensor_tensor(out=r(7), in0=r(8), scalar=-3.0e38, in1=es, op0=ALU.mult, op1=ALU.add))
            do(first_max(r(7), EPG, r(9, 1), r(12), r(2, 1), r(13)))
            v_.tensor_tensor(r(10, 1), r(9, 1), r(6, 1), ALU.subtract).then_inc(r_sub, 1)
            ve.wait_ge(r_exp, 2)
            do(v_.tensor_reduce(r(14, 1), r(4, NG), AX, ALU.add))
            do(v_.tensor_scalar(r(15, 1), r(11, 1), 1.0, None, ALU.add))
            do(v_.tensor_tensor(r(14, 1), r(14, 1), r(15, 1), ALU.mult))
            do(v_.reciprocal(r(14, 1), r(14, 1)))
            do(v_.tensor_tensor(r(15, 1), r(14, 1), r(11, 1), ALU.mult))
            do(v_.tensor_tensor(r(8), r(8), wide(r(14, 1), 8), ALU.mult))
            do(v_.tensor_tensor(r(13), r(13), wide(r(15, 1), 8), ALU.mult))
            do(v_.tensor_tensor(r(8), r(8), r(13), ALU.add))
            for t in range(NT):
                add(v_.tensor_tensor(comb[:, t, :].rearrange("p (g e) -> p g e", g=NG),
                                     onehot[:, t, :].unsqueeze(2).broadcast_to([P, NG, EPG]),
                                     rt[:, 8, t, :].unsqueeze(1).broadcast_to([P, NG, EPG]), ALU.mult))
            ve.wait_ge(rank_bank, 1)
            do(v_.tensor_tensor(rank[:, :, :], bank[5][:, 0:NT * NG].rearrange("p (t g) -> p t g", t=NT),
                                onehot[:, :, :], ALU.mult))
            do(v_.tensor_scalar(rank[:, :, :], rank[:, :, :], -1.0, None, ALU.add))
            do(v_.tensor_reduce(cnt[:, :], bank[5][:, NT * NG:(NT + 1) * NG], AX, ALU.max))
            v_.tensor_scalar(flag[:, :], cnt[:, :], float(P), None, ALU.is_gt).then_inc(route_ok, 1)

            def one_hots(g):
                for t in range(NT):
                    rk = rank[:, t, bass.ds(g, 1)]
                    add(v_.tensor_scalar(hot[:, t, :], iota[:, :], rk, None, ALU.is_equal))
                    ins = v_.tensor_scalar(hot_s[:, t, :], iota[:, :], rk, stat[:, 4 + t:5 + t], ALU.is_equal, ALU.mult)
                    if t == 0:
                        add(ins)
                ins.then_inc(g_hot, 1)

            HOT_ADDS, ROWS_ADDS, EXPERT_ADDS = 3, 8, 2

            def take_rows_gathered(n, scattered):
                for q in range(4):
                    ve.wait_ge(g_bank, n * 4 + (q + 1))
                    if q:
                        ve.wait_ge(g_out, n * 4 + q)
                    else:
                        ve.wait_ge(sc_out, scattered)
                    for j in range(4):
                        k = 4 * q + j
                        ins = v_.tensor_scalar(tmp[:, j * P:(j + 1) * P], bank[7 - q % 2][:, j * P:(j + 1) * P],
                                               cols[:, C_A2, k:k + 1], cols[:, C_S2, k:k + 1], ALU.mult, ALU.add)
                    add(ins)
                    wait()
                    chunks = slice(4 * q, 4 * q + 4)
                    raw = tmp.rearrange("p (j s) -> p j s", j=4)
                    add(v_.tensor_copy(hG_hi[:, chunks, :], raw))
                    wait()
                    v_.tensor_tensor(hG_lo[:, chunks, :], raw, hG_hi[:, chunks, :].bitcast(F32), ALU.subtract
                                     ).then_inc(g_out, 1)

            def take_routing(n):
                ve.wait_ge(g_hotT, n + 1)
                v_.tensor_copy(hotT, bank[6][:, 0:SEQ])
                v_.tensor_copy(comb_s, bank[6][:, SEQ:SEQ + EPG]).then_inc(g_hotT_out, 1)

            def expert(e, ne, following=True):
                for h in range(LEAD, 16 + LEAD if following else 16):
                    remainder_moe(ne, h)
                    if h == 13:
                        ve.wait_ge(e_exp, ne * 2 + 2)
                        add(v_.reciprocal(act_t, act_e))
                        wait()
                        add(v_.tensor_tensor(act_t, act_t, bank[4][:, :], ALU.mult))
                wait()
                ve.wait_ge(split_used, ne * 16 + (CREDIT + K_MOE + 16))
                ve.wait_ge(e_tr, CREDIT + ne)
                v_.scalar_tensor_tensor(out=act_o, in0=bank[5][:, :], scalar=comb_s[:, bass.ds(e, 1)], in1=act_t,
                                        op0=ALU.mult, op1=ALU.mult).then_inc(e_act, 1)

            def take_scatter(n):
                for t in range(NT):
                    for q in range(4):
                        ve.wait_ge(sc_bank, n * 8 + (4 * t + q + 1))
                        ve.wait_ge(sc_out, CREDIT + n * 8 + (4 * t + q))
                        add(v_.tensor_tensor(tmp, bank[q][:, :], gt2[:, q * 512:(q + 1) * 512], ALU.mult))
                        wait()
                        xs = x1[:, t, q * 512:(q + 1) * 512]
                        v_.tensor_tensor(xs, xs, tmp, ALU.add).then_inc(sc_out, 1)

            def group(g, n, ne, following):
                ve.wait_ge(g_hotT_out, n + 1)
                if following:
                    one_hots(g + 1)
                start, count = own.start, own.n
                with ve.Fori(0, EPG - 1) as e:
                    own.start, own.n = start + count + e * EXPERT_ADDS, 0
                    expert(e, ne + e)
                    assert own.n == EXPERT_ADDS
                own.start, own.n = start, count + (EPG - 1) * EXPERT_ADDS
                expert(EPG - 1, ne + (EPG - 1), following)
                if following:
                    take_rows_gathered(n + 1, n * 8 + CREDIT)
                    ve.wait_ge(g_out, n * 4 + 8)
                take_scatter(n)
                if following:
                    take_routing(n + 1)

            GROUP_ADDS = HOT_ADDS + EXPERT_ADDS * EPG + ROWS_ADDS + 8

            def moe_pass(ps):
                n0 = ps * NG
                if ps:
                    do(v_.tensor_scalar(rank[:, :, :], rank[:, :, :], -float(P), None, ALU.add))
                one_hots(0)
                take_rows_gathered(n0, n0 * 8 + CREDIT)
                take_routing(n0)
                with ve.Fori(0, NG - 1) as g:
                    own.enter(g, GROUP_ADDS)
                    saved = own.outer
                    group(g, g + n0, g * EPG + n0 * EPG, True)
                    own.outer = saved
                    own.leave(NG - 1, GROUP_ADDS)
                group(NG - 1, n0 + NG - 1, (n0 + NG - 1) * EPG, False)

            moe_pass(0)
            ve.wait_ge(route_ok, 1)
            over = ve.value_load(flag[0:1, 0:1], min_val=0, max_val=1)
            with ve.If(over > 0):
                for h in range(LEAD):
                    remainder_moe(NE, h)
                moe_pass(1)

_INS = ["x", "c", "w_ada", "b_ada", "ln1_g", "w_in", "swa_q_norm", "swa_k_norm", "swa_sinks", "dsa_q_norm",
        "dsa_k_norm", "w_branch_a", "w_branch_b", "w_out", "ln2_g", "w_group", "b_group", "w_expert", "b_expert",
        "w_gate_up", "w_up", "w_down"]


def kernel(**inputs):
    import concourse.bacc as bacc
    from concourse.bass_utils import run_bass_kernel_spmd

    nc = bacc.Bacc("TRN2", target_bir_lowering=False, num_devices=1)
    arrays, args = {}, []
    for name in _INS:
        a = np.ascontiguousarray(inputs[name])
        arrays[f"in_{name}"] = a
        args.append(nc.dram_tensor(f"in_{name}", a.shape, mybir.dt.from_np(a.dtype), kind="ExternalInput").ap())
    args.append(nc.dram_tensor("out_x", (1, SEQ, D), F32, kind="ExternalOutput").ap())
    decoder_block(nc, *args)
    r = run_bass_kernel_spmd(nc, [arrays], core_ids=[0])
    return r.results[0]["out_x"]
```
